# Optimizing a Trainium2 kernel written in Bass

```python
import math
import jax, jax.numpy as jnp
from jax import lax
import numpy as np

D_MODEL = 1024
BATCH = 1
SEQ = 512
DEPTH = 2

N_A_LAYERS = DEPTH // 2
N_B_LAYERS = DEPTH - N_A_LAYERS
NORM_EPS = 1e-6

RWKV_HEAD = 64
RWKV_HEADS = D_MODEL // RWKV_HEAD
RWKV_DECAY_LORA = 64
RWKV_AAA_LORA = 64
RWKV_GATE_LORA = 160
RWKV_GN_EPS = 64e-5

NSA_HEADS = 16
NSA_KV_GROUPS = 4
NSA_HPG = NSA_HEADS // NSA_KV_GROUPS
NSA_HEAD_DIM = D_MODEL // NSA_HEADS
NSA_KV_PARTS = 6
CMP_BLOCK = 32
CMP_STRIDE = 16
CMP_HIDDEN = 256
SEL_BLOCK = 64
SEL_TOPK = 8
WINDOW = 512
Q_CHUNK = 32
N_BRANCH = 3
IMP_FORCE = 1e4

REL_BUCKETS = 32
REL_MAX_DIST = 128

MOE_GROUPS = 4
MOE_EXPERTS_PER_GROUP = 8
MOE_EXPERTS = MOE_GROUPS * MOE_EXPERTS_PER_GROUP
MOE_TOPK = 2
MOE_HIDDEN = 512
MOE_BLOCK = 128

kernel_name = 'hybrid_rwkv7_nsa_hmoe_yoco'

def rms_norm(x, g):
    xf = x.astype(jnp.float32)
    y = xf * lax.rsqrt(jnp.mean(xf * xf, axis=-1, keepdims=True) + NORM_EPS)
    return (y * g.astype(jnp.float32)).astype(x.dtype)

def rel_bucket(dist):
    n = jnp.maximum(dist, 0)
    max_exact = REL_BUCKETS // 2
    nf = jnp.maximum(n, 1).astype(jnp.float32)
    large = max_exact + (jnp.log(nf / max_exact) / math.log(REL_MAX_DIST / max_exact)
                         * (REL_BUCKETS - max_exact)).astype(jnp.int32)
    large = jnp.minimum(large, REL_BUCKETS - 1)
    return jnp.where(n < max_exact, n, large)

def masked_softmax(logits, mask):
    logits = jnp.where(mask, logits, -1e30)
    m = jnp.max(logits, axis=-1, keepdims=True)
    p = jnp.exp(logits - m) * mask
    return p / jnp.maximum(jnp.sum(p, axis=-1, keepdims=True), 1e-30)

def rwkv7_time_mix(x, mu, w_r, w_k, w_v, w_o, w0, w1, w2, a0, a1, a2, g1, g2,
                   k_k, k_a, r_k, lnx_w, lnx_b):
    b, t, c = x.shape
    f32 = jnp.float32
    hshape = (b, t, RWKV_HEADS, RWKV_HEAD)
    xx = jnp.pad(x, ((0, 0), (1, 0), (0, 0)))[:, :-1] - x
    xr, xw, xk, xv, xa, xg = (x + xx * mu[i] for i in range(6))
    r = xr @ w_r
    k = xk @ w_k
    v = xv @ w_v
    w = -jax.nn.softplus(-(w0 + jnp.tanh(xw @ w1) @ w2)) - 0.5
    a = jax.nn.sigmoid(a0 + (xa @ a1) @ a2)
    g = jax.nn.sigmoid(xg @ g1) @ g2
    kk = (k * k_k).reshape(hshape).astype(f32)
    kk = kk * lax.rsqrt(jnp.maximum(jnp.sum(kk * kk, -1, keepdims=True), 1e-24))
    k = k * (1.0 + (a - 1.0) * k_a)
    decay = jnp.exp(-jnp.exp(w.astype(f32)))
    r_h = r.reshape(hshape).astype(f32)
    k_h = k.reshape(hshape).astype(f32)
    v_h = v.reshape(hshape).astype(f32)
    a_h = a.reshape(hshape).astype(f32)

    def to_time(z):
        return jnp.moveaxis(z.reshape(hshape).astype(f32), 1, 0)

    xs = (to_time(r_h), to_time(decay), to_time(k_h), to_time(v_h),
          to_time(-kk), to_time(kk * a_h))

    def step(state, inp):
        r_t, w_t, k_t, v_t, a_t, b_t = inp
        sa = jnp.einsum('bhij,bhj->bhi', state, a_t)
        state = (state * w_t[:, :, None, :] + sa[..., None] * b_t[:, :, None, :]
                 + v_t[..., None] * k_t[:, :, None, :])
        return state, jnp.einsum('bhij,bhj->bhi', state, r_t)

    s0 = jnp.zeros((b, RWKV_HEADS, RWKV_HEAD, RWKV_HEAD), f32)
    _, y = lax.scan(step, s0, xs)
    y = jnp.moveaxis(y, 0, 1)
    mean = jnp.mean(y, -1, keepdims=True)
    var = jnp.mean(jnp.square(y - mean), -1, keepdims=True)
    y = ((y - mean) * lax.rsqrt(var + RWKV_GN_EPS)).reshape(b, t, c)
    y = y * lnx_w.astype(f32) + lnx_b.astype(f32)
    bonus = jnp.sum(r_h * k_h * r_k.astype(f32), -1, keepdims=True) * v_h
    y = y + bonus.reshape(b, t, c)
    return (y * g.astype(f32)).astype(x.dtype) @ w_o

def nsa_shared_kv(h, kv_ln, kv_w, cmp_pe_k, cmp_pe_v, cmp_k_w1, cmp_k_w2, cmp_v_w1, cmp_v_w2):
    b, t, _ = h.shape
    G, dh = NSA_KV_GROUPS, NSA_HEAD_DIM
    hn = rms_norm(h, kv_ln)
    kv = (hn @ kv_w).reshape(b, t, NSA_KV_PARTS, G, dh)
    kv = jnp.moveaxis(kv, 1, 3)
    k_cr, v_cr, k_sel, v_sel, k_win, v_win = (kv[:, i] for i in range(NSA_KV_PARTS))
    n_cmp = (t - CMP_BLOCK) // CMP_STRIDE + 1
    blk_idx = jnp.arange(n_cmp)[:, None] * CMP_STRIDE + jnp.arange(CMP_BLOCK)[None, :]

    def compress(z, pe, w1, w2):
        zb = z[:, :, blk_idx] + pe[:, None]
        zb = zb.reshape(b, G, n_cmp, CMP_BLOCK * dh)
        return jax.nn.gelu(zb @ w1) @ w2

    k_cmp = compress(k_cr, cmp_pe_k, cmp_k_w1, cmp_k_w2)
    v_cmp = compress(v_cr, cmp_pe_v, cmp_v_w1, cmp_v_w2)
    n_sel = t // SEL_BLOCK
    k_sel = k_sel.reshape(b, G, n_sel, SEL_BLOCK, dh)
    v_sel = v_sel.reshape(b, G, n_sel, SEL_BLOCK, dh)
    return k_cmp, v_cmp, k_sel, v_sel, k_win, v_win

def nsa_attention(hn, w_qg, w_o, rel_bias, k_cmp, v_cmp, k_sel, v_sel, k_win, v_win):
    b, t, _ = hn.shape
    f32 = jnp.float32
    G, HPG, dh = NSA_KV_GROUPS, NSA_HPG, NSA_HEAD_DIM
    qg = hn @ w_qg
    q = qg[..., :NSA_HEADS * dh].reshape(b, t, G, HPG, dh).transpose(0, 2, 3, 1, 4)
    gates = jax.nn.sigmoid(qg[..., NSA_HEADS * dh:].astype(f32))
    gates = gates.reshape(b, t, G, HPG, N_BRANCH).transpose(0, 2, 3, 1, 4)
    table = rel_bias.astype(f32).reshape(REL_BUCKETS, G, HPG).transpose(1, 2, 0)
    n_cmp = k_cmp.shape[2]
    n_sel = k_sel.shape[2]
    topk = min(SEL_TOPK, n_sel)
    cmp_start = jnp.arange(n_cmp) * CMP_STRIDE
    cmp_end = cmp_start + CMP_BLOCK - 1
    sel_start = jnp.arange(n_sel) * SEL_BLOCK
    overlap = ((cmp_start[:, None] < sel_start[None, :] + SEL_BLOCK)
               & (cmp_start[:, None] + CMP_BLOCK > sel_start[None, :])).astype(f32)
    k_win_p = jnp.pad(k_win, ((0, 0), (0, 0), (WINDOW, 0), (0, 0)))
    v_win_p = jnp.pad(v_win, ((0, 0), (0, 0), (WINDOW, 0), (0, 0)))
    scale = NSA_HEAD_DIM ** -0.5
    g_idx = jnp.arange(G)[None, :, None, None, None]
    h_idx = jnp.arange(HPG)[None, None, :, None, None]
    gather_blocks = jax.vmap(jax.vmap(lambda blocks, ix: blocks[ix]))

    def chunk(c):
        t0 = c * Q_CHUNK
        tq = t0 + jnp.arange(Q_CHUNK)
        qc = lax.dynamic_slice_in_dim(q, t0, Q_CHUNK, axis=3)
        gc = lax.dynamic_slice_in_dim(gates, t0, Q_CHUNK, axis=3)
        lc = (jnp.einsum('bghqd,bgkd->bghqk', qc, k_cmp).astype(f32) * scale
              + table[:, :, rel_bucket(tq[:, None] - cmp_end[None, :])])
        pc = masked_softmax(lc, cmp_end[None, :] <= tq[:, None])
        oc = jnp.einsum('bghqk,bgkd->bghqd', pc.astype(v_cmp.dtype), v_cmp)
        imp = jnp.einsum('bghqk,kj->bgqj', pc, overlap)
        blk_q = (tq // SEL_BLOCK)[:, None]
        jj = jnp.arange(n_sel)[None, :]
        forced = (jj == 0) | (jj == blk_q) | (jj == blk_q - 1)
        score = jnp.where(forced, IMP_FORCE, jnp.where(jj <= blk_q, imp, -1.0))
        _, idx = lax.top_k(score, topk)
        ks = gather_blocks(k_sel, idx).reshape(b, G, Q_CHUNK, topk * SEL_BLOCK, dh)
        vs = gather_blocks(v_sel, idx).reshape(b, G, Q_CHUNK, topk * SEL_BLOCK, dh)
        pos = (idx[..., None] * SEL_BLOCK + jnp.arange(SEL_BLOCK)).reshape(b, G, Q_CHUNK, topk * SEL_BLOCK)
        bias_s = table[g_idx, h_idx, rel_bucket(tq[:, None] - pos)[:, :, None]]
        ls = jnp.einsum('bghqd,bgqkd->bghqk', qc, ks).astype(f32) * scale + bias_s
        ps = masked_softmax(ls, (pos <= tq[:, None])[:, :, None])
        o_sel = jnp.einsum('bghqk,bgqkd->bghqd', ps.astype(vs.dtype), vs)
        kw = lax.dynamic_slice_in_dim(k_win_p, t0, WINDOW + Q_CHUNK, axis=2)
        vw = lax.dynamic_slice_in_dim(v_win_p, t0, WINDOW + Q_CHUNK, axis=2)
        kp = t0 - WINDOW + jnp.arange(WINDOW + Q_CHUNK)
        dist = tq[:, None] - kp[None, :]
        mask_w = (dist >= 0) & (dist < WINDOW) & (kp[None, :] >= 0)
        lw = (jnp.einsum('bghqd,bgkd->bghqk', qc, kw).astype(f32) * scale
              + table[:, :, rel_bucket(dist)])
        pw = masked_softmax(lw, mask_w)
        ow = jnp.einsum('bghqk,bgkd->bghqd', pw.astype(vw.dtype), vw)
        out = gc[..., 0:1] * oc + gc[..., 1:2] * o_sel + gc[..., 2:3] * ow
        return out.astype(hn.dtype)

    o = lax.map(chunk, jnp.arange(t // Q_CHUNK))
    o = o.transpose(1, 0, 4, 2, 3, 5).reshape(b, t, NSA_HEADS * dh)
    return o @ w_o

def hier_moe(h, ln_g, w_gr, b_gr, w_er, b_er, w1, w3, w2):
    bt, t, c = h.shape
    n = bt * t
    f32 = jnp.float32
    xf = rms_norm(h, ln_g).reshape(n, c)
    gp = jax.nn.softmax((xf @ w_gr).astype(f32) + b_gr.astype(f32), axis=-1)
    grp_w, grp = lax.top_k(gp, 1)
    el = ((xf @ w_er).astype(f32) + b_er.astype(f32)).reshape(n, MOE_GROUPS, MOE_EXPERTS_PER_GROUP)
    el = jnp.take_along_axis(el, grp[:, :, None], axis=1)[:, 0]
    ew, ei = lax.top_k(jax.nn.softmax(el, axis=-1), MOE_TOPK)
    weight = grp_w * ew / jnp.sum(ew, -1, keepdims=True)
    expert = grp * MOE_EXPERTS_PER_GROUP + ei
    n_as = n * MOE_TOPK
    flat_e = expert.reshape(n_as)
    flat_t = jnp.repeat(jnp.arange(n), MOE_TOPK)
    flat_w = weight.reshape(n_as)
    order = jnp.argsort(flat_e)
    se, st, sw = flat_e[order], flat_t[order], flat_w[order]
    counts = jnp.bincount(flat_e, length=MOE_EXPERTS)
    starts = jnp.cumsum(counts) - counts
    pcounts = (counts + MOE_BLOCK - 1) // MOE_BLOCK * MOE_BLOCK
    pend = jnp.cumsum(pcounts)
    pstarts = pend - pcounts
    dest = pstarts[se] + jnp.arange(n_as) - starts[se]
    p = n_as + MOE_EXPERTS * MOE_BLOCK
    n_blk = p // MOE_BLOCK
    buf_t = jnp.zeros((p,), jnp.int32).at[dest].set(st)
    buf_w = jnp.zeros((p,), f32).at[dest].set(sw)
    blk_e = jnp.clip(jnp.searchsorted(pend, jnp.arange(n_blk) * MOE_BLOCK, side='right'), 0, MOE_EXPERTS - 1)
    xbuf = xf[buf_t].reshape(n_blk, MOE_BLOCK, c)

    def expert_block(args):
        xb, e = args
        return (jax.nn.silu(xb @ w1[e]) * (xb @ w3[e])) @ w2[e]

    yb = lax.map(expert_block, (xbuf, blk_e)).reshape(p, c)
    y = jnp.zeros((n, c), yb.dtype).at[buf_t].add(yb * buf_w[:, None].astype(yb.dtype))
    return y.reshape(bt, t, c)

def setup_inputs(seed: int = 0) -> dict:
    key = jax.random.key(seed)
    ks = iter(jax.random.split(key, 64))
    f32 = jnp.float32
    D = D_MODEL
    NA, NB = N_A_LAYERS, N_B_LAYERS
    G, dh, H = NSA_KV_GROUPS, NSA_HEAD_DIM, NSA_HEADS

    def nrm(shape, scale):
        return jax.random.normal(next(ks), shape, f32) * scale

    def gain(shape):
        return 1.0 + nrm(shape, 0.05)

    frac = jnp.arange(D, dtype=f32) / (D - 1)
    inp = {}
    inp['x'] = nrm((BATCH, SEQ, D), 1.0)
    inp['a_ln'] = gain((NA, D))
    inp['a_mu'] = jax.random.uniform(next(ks), (NA, 6, D), f32)
    inp['a_wr'] = nrm((NA, D, D), D ** -0.5)
    inp['a_wk'] = nrm((NA, D, D), D ** -0.5)
    inp['a_wv'] = nrm((NA, D, D), D ** -0.5)
    inp['a_wo'] = nrm((NA, D, D), D ** -0.5)
    inp['a_w0'] = (-6.5 + 5.0 * frac ** 0.85)[None] + nrm((NA, D), 0.1)
    inp['a_w1'] = nrm((NA, D, RWKV_DECAY_LORA), D ** -0.5)
    inp['a_w2'] = nrm((NA, RWKV_DECAY_LORA, D), 0.1 * RWKV_DECAY_LORA ** -0.5)
    inp['a_a0'] = nrm((NA, D), 0.1)
    inp['a_a1'] = nrm((NA, D, RWKV_AAA_LORA), D ** -0.5)
    inp['a_a2'] = nrm((NA, RWKV_AAA_LORA, D), 0.5 * RWKV_AAA_LORA ** -0.5)
    inp['a_g1'] = nrm((NA, D, RWKV_GATE_LORA), D ** -0.5)
    inp['a_g2'] = nrm((NA, RWKV_GATE_LORA, D), RWKV_GATE_LORA ** -0.5)
    inp['a_kk'] = 0.85 + nrm((NA, D), 0.05)
    inp['a_ka'] = gain((NA, D))
    inp['a_rk'] = nrm((NA, RWKV_HEADS, RWKV_HEAD), 0.1)
    inp['a_lnx_w'] = gain((NA, D))
    inp['a_lnx_b'] = nrm((NA, D), 0.01)
    inp['kv_ln'] = gain((D,))
    inp['kv_w'] = nrm((D, NSA_KV_PARTS * G * dh), D ** -0.5)
    inp['cmp_pe_k'] = nrm((G, CMP_BLOCK, dh), 0.5)
    inp['cmp_pe_v'] = nrm((G, CMP_BLOCK, dh), 0.5)
    inp['cmp_k_w1'] = nrm((CMP_BLOCK * dh, CMP_HIDDEN), (CMP_BLOCK * dh) ** -0.5)
    inp['cmp_k_w2'] = nrm((CMP_HIDDEN, dh), CMP_HIDDEN ** -0.5)
    inp['cmp_v_w1'] = nrm((CMP_BLOCK * dh, CMP_HIDDEN), (CMP_BLOCK * dh) ** -0.5)
    inp['cmp_v_w2'] = nrm((CMP_HIDDEN, dh), CMP_HIDDEN ** -0.5)
    inp['rel_bias'] = nrm((REL_BUCKETS, H), 0.5)
    inp['b_ln'] = gain((NB, D))
    inp['b_wqg'] = nrm((NB, D, H * dh + N_BRANCH * H), D ** -0.5)
    inp['b_wo'] = nrm((NB, H * dh, D), (H * dh) ** -0.5)
    inp['m_ln'] = gain((DEPTH, D))
    inp['m_wg'] = nrm((DEPTH, D, MOE_GROUPS), D ** -0.5)
    inp['m_bg'] = nrm((DEPTH, MOE_GROUPS), 0.01)
    inp['m_we'] = nrm((DEPTH, D, MOE_EXPERTS), D ** -0.5)
    inp['m_be'] = nrm((DEPTH, MOE_EXPERTS), 0.01)
    inp['m_w1'] = nrm((DEPTH, MOE_EXPERTS, D, MOE_HIDDEN), D ** -0.5)
    inp['m_w3'] = nrm((DEPTH, MOE_EXPERTS, D, MOE_HIDDEN), D ** -0.5)
    inp['m_w2'] = nrm((DEPTH, MOE_EXPERTS, MOE_HIDDEN, D), MOE_HIDDEN ** -0.5)
    inp['final_ln'] = gain((D,))
    return inp

def reference(x, a_ln, a_mu, a_wr, a_wk, a_wv, a_wo, a_w0, a_w1, a_w2, a_a0, a_a1, a_a2,
              a_g1, a_g2, a_kk, a_ka, a_rk, a_lnx_w, a_lnx_b,
              kv_ln, kv_w, cmp_pe_k, cmp_pe_v, cmp_k_w1, cmp_k_w2, cmp_v_w1, cmp_v_w2,
              rel_bias, b_ln, b_wqg, b_wo,
              m_ln, m_wg, m_bg, m_we, m_be, m_w1, m_w3, m_w2, final_ln):
    h = x
    shared = None
    for layer in range(DEPTH):
        if layer < N_A_LAYERS:
            i = layer
            h = h + rwkv7_time_mix(rms_norm(h, a_ln[i]), a_mu[i], a_wr[i], a_wk[i], a_wv[i], a_wo[i],
                                   a_w0[i], a_w1[i], a_w2[i], a_a0[i], a_a1[i], a_a2[i],
                                   a_g1[i], a_g2[i], a_kk[i], a_ka[i], a_rk[i], a_lnx_w[i], a_lnx_b[i])
        else:
            j = layer - N_A_LAYERS
            if j == 0:
                shared = nsa_shared_kv(h, kv_ln, kv_w, cmp_pe_k, cmp_pe_v,
                                       cmp_k_w1, cmp_k_w2, cmp_v_w1, cmp_v_w2)
            k_cmp, v_cmp, k_sel, v_sel, k_win, v_win = shared
            h = h + nsa_attention(rms_norm(h, b_ln[j]), b_wqg[j], b_wo[j], rel_bias,
                                  k_cmp, v_cmp, k_sel, v_sel, k_win, v_win)
        h = h + hier_moe(h, m_ln[layer], m_wg[layer], m_bg[layer], m_we[layer], m_be[layer],
                         m_w1[layer], m_w3[layer], m_w2[layer])
    return rms_norm(h, final_ln)


_drawn_inputs = setup_inputs


def setup_inputs(seed=0):
    import zlib

    import numpy as np

    out = dict(_drawn_inputs(seed))
    spreads = {}
    factors = {'a_w1': 7.686,
     'm_bg': 3.898,
     'a_w2': 3.637,
     'a_lnx_b': 3.01,
     'kv_ln': 3.344,
     'b_ln': 3.285}
    for name, (base, spread) in spreads.items():
        noise = np.random.default_rng([zlib.crc32(name.encode()), seed]).standard_normal(out[name].shape)
        drawn = base * np.exp(spread * noise) if base else spread * noise
        out[name] = __import__('jax').numpy.asarray(drawn.astype(out[name].dtype))
    for name, factor in factors.items():
        out[name] = (out[name] * factor).astype(out[name].dtype)
    return out
```

```python
import concourse.bass as bass
from concourse import mybir
from contextlib import ExitStack

FP32 = mybir.dt.float32
I32 = mybir.dt.int32
ALU = mybir.AluOpType
ACT = mybir.ActivationFunctionType
AX = mybir.AxisListType

P = 128
D = 1024
T = 512
NJ = T // P
NK = D // P
EPS = 1e-6
HD = 64
C = 64
NC = T // C
NP = 8
PACKS = NC * NP
GN_EPS = 64e-5
DECAY = 0.6065306597126334

E = 32
HID = 512
CAP = 64
OVER = 15
SLOTS = (E + OVER) * CAP
NG, HPG, NH = 4, 4, 16
NCMP = 31
NEG = -1e30
U = 4096

VEC_P = ["a_ln", "mu0", "mu1", "mu2", "mu3", "mu4", "mu5", "kv_ln", "b_ln", "m_ln0", "m_ln1"]
VEC_M = ["w0", "a0", "kk", "ka", "rk", "lnx_w", "lnx_b"]
CONST = [("ident", 128), ("head_ones", 128), ("upper32", 128), ("upper64", 128), ("upper_incl", 128),
         ("lower32", 128), ("lower_off", 128), ("scan_keep", 512), ("before", 128), ("ones", 128),
         ("head_mask", 128), ("iota", 32), ("iota_over", 16), ("thresholds", 8), ("slot0", 32), ("token_id", 4)]


def offsets(pairs):
    at, out = 0, {}
    for name, n in pairs:
        out[name] = (at, n)
        at += n
    return out, at


CONST_AT, CONST_N = offsets(CONST)
VEC_AT, VEC_N = offsets([(v, 8) for v in VEC_P + VEC_M])

GOES_ON = {
    "S_mm": ("pe_g", PACKS), "probs_mm": ("pe_sq", PACKS), "O_mm": ("pe_l1", PACKS), "oT_mm": ("pe_l2", PACKS),
    "b_wo_mm": ("pe_l3", PACKS), "cS_mm": ("pe_l4", PACKS), "cT_mm": ("pe_mz", PACKS), "cO_mm": ("pe_mx", PACKS),
    "cmp_hidden": ("pe_rh", PACKS), "cmp_out": ("pe_u", PACKS), "gate_mm": ("pe_y", PACKS),
    "q_mm": ("pe_tr", PACKS), "bias_mm": ("pe_s", PACKS), "kv_mm": ("lora_mm", 3 * NP),
    "router_mm": ("k_ssq", NP), "place_mm": ("bonus_mm", NP),
    "probs_ready": ("ev_l1", PACKS), "pT_act": ("ev_l2", PACKS), "oT_act": ("ev_l3", PACKS),
    "cexp": ("ev_mz", PACKS), "cT_ready": ("ev_rh", PACKS), "cmp_act": ("ev_tr", PACKS),
    "gates_ready": ("ev_sq", PACKS), "kcmp_ready": ("ev_y", PACKS), "q_act": ("k_sq", NP),
    "rev_ev": ("k_norm", NP), "kv_act": ("k_factor", NP),
    "biased": ("ev_g", PACKS), "pT_dve": ("ev_x1", PACKS), "o_added": ("ev_x2", PACKS), "oT_dve": ("ev_x3", PACKS),
    "cshifted": ("ev_x4", PACKS), "cprobs_ready": ("ev_mx", PACKS), "cO_ev": ("ev_late", PACKS),
    "vcmp_ready": ("ev_u", PACKS), "blocks_ready": ("ev_s", PACKS), "q_dve": ("k_rnorm", NP),
    "kv_dve": ("kk_ready", NP), "rel_mask": ("k_scaled", NP),
    "q_w_in": ("lora1_in", 48), "kv_w_in": ("lora2_in", 64), "b_wo_in": ("x_in", 16), "gate_w_in": ("vec_in", 16),
    "bias_in": ("const_in", 16), "cmp_w2_in": ("y_clear", 32), "cmp_pe_in": ("table_clear", 32),
    "cmp_w1_in": ("router_in", 32),
} | {f"bias_h{i}": (f"wring{i}", 128) for i in range(4)}


def spread(ap, axis, n):
    ap = ap.unsqueeze(axis)
    return ap.broadcast_to([*ap.shape[:axis], n, *ap.shape[axis + 1:]])


def decoder_program(nc, d, out):
    stack = ExitStack()
    with stack:
        def sb(name, shape, dt=FP32):
            return stack.enter_context(nc.sbuf_tensor(name, shape, dt))

        sems = {}

        def sem(name):
            name = GOES_ON.get(name, (name, 0))[0]
            if name not in sems:
                sems[name] = stack.enter_context(nc.semaphore(name))
            return sems[name]

        def at(name, count):
            return count + GOES_ON.get(name, (name, 0))[1]

        arena = sb("arena", [P, 12 * U])

        def region(i, n=U):
            return arena[:, i * U:i * U + n]

        ints = sb("ints", [P, 144], I32)
        const = sb("const", [P, CONST_N])
        vec = sb("vec", [P, VEC_N])
        small = sb("small", [P, 512])
        state = sb("state", [P, NP, P])

        def cst(name):
            at, n = CONST_AT[name]
            return const[:, at:at + n]

        def v8(name):
            at, n = VEC_AT[name]
            return vec[:, at:at + n]

        ident = cst("ident")
        head_ones = cst("head_ones")
        bank = [stack.enter_context(nc.psum_tensor(f"bank{i}", [P, 512], FP32)) for i in range(8)]

        h = region(0).rearrange("p (j c) -> p j c", j=NJ)
        xT = region(1).rearrange("p (k t) -> p k t", k=NK)
        xxT = region(2).rearrange("p (k t) -> p k t", k=NK)
        mix = region(3).rearrange("p (s t) -> p s t", s=8)
        wring = region(4).rearrange("p (s n) -> p s n", s=4)
        r_T, a_T, b_T, k_T, v_T, g_T, l_T = (region(i).rearrange("p (m t) -> p m t", m=NP) for i in range(5, 12))
        ra_T = arena[:, 5 * U:7 * U].rearrange("p (w m t) -> p w m t", w=2, m=NP)
        y_T = region(1).rearrange("p (m t) -> p m t", m=NP)
        xn = region(5).rearrange("p (j c) -> p j c", j=NJ)
        w1l = region(6)[:, 0:512].rearrange("p (k n) -> p k n", k=NK)
        a1l = region(6)[:, 512:1024].rearrange("p (k n) -> p k n", k=NK)
        g1l = region(6)[:, 1024:2304].rearrange("p (k n) -> p k n", k=NK)
        w2l, a2l, g2l, g2r = (region(8)[:, 1024 * i:1024 * i + 1024] for i in range(4))
        hid_w, hid_a, hid_g, hid_r = (region(9)[:, 512 * i:512 * i + 512] for i in range(4))
        sig = region(9)[:, 2048:3072].rearrange("p (s t) -> p s t", s=2)
        tmp = region(2).rearrange("p (x s t) -> p x s t", x=4, s=2)

        sumsq, rstd = small[:, 0:4], small[:, 4:8]
        one_ka = small[:, 8:16]
        chunk_decay = small[:, 16:80].rearrange("p (m c) -> p m c", m=NP)

        stage_at = [2 * U]

        def stage(depth, n):
            a = stage_at[0]
            stage_at[0] += depth * n
            assert stage_at[0] <= 5 * U
            return arena[:, a:a + depth * n].rearrange("p (s n) -> p s n", s=depth)

        ab_e = stage(2, 256)
        bkv_e = stage(2, 384)
        a_e = stage(4, 128)
        at32 = stage(2, 128)
        a32 = stage(2, 128)
        a_off = stage(8, 128)
        lv = [None, stage(2, 384), stage(2, 384), stage(2, 384), stage(2, 256)]
        x4 = stage(4, 128)
        tz = stage(2, 256)
        x_all = stage(4, 128)
        ak_t = stage(4, 128)
        rbk = stage(4, 128)
        bkv_s = stage(4, 384)
        rhs_s = stage(2, 128)
        u_s = stage(4, 128)
        s_dec = stage(2, 128)
        p_g, p_a, p_rh = bank[0][:, 0:64], bank[0][:, 64:192], bank[0][:, 256:384]
        p_sq, p_u = bank[1][:, 0:256], bank[1][:, 256:384]
        p_l1, p_l2 = bank[2][:, 0:384], bank[3][:, 0:384]
        p_l3, p_y = bank[4][:, 0:256], bank[4][:, 256:320]
        p_l4, p_tr = bank[5][:, 0:128], bank[5][:, 128:512]
        p_mz, p_late = bank[6][:, 0:256], bank[6][:, 256:448]
        p_mx, p_s = bank[7][:, 0:128], bank[7][:, 128:256]

        def upto(n):
            return min(n, PACKS - 1) + 1

        def last_of(tick, stages):
            return next(((name, tick - off) for name, off in reversed(stages) if 0 <= tick - 1 - off < PACKS),
                        (None, 0))

        wo_rows = d["a_wo"].rearrange("(m p) n -> m p n", p=P)

        w_slot = [[region(i) for i in regs] for regs in ((7, 8, 9), (10, 11, 6), (3, 4, 5))]
        w13_slot = [arena[:, i * U:(i + 2) * U].rearrange("p (w k n) -> p w k n", w=2, k=NK) for i in (7, 10, 3)]
        xn_m = region(1).rearrange("p (j c) -> p j c", j=NJ)
        xT_m = region(2).rearrange("p (k t) -> p k t", k=NK)
        xg = region(1)[0:CAP, 0:2048].rearrange("p (s c) -> p s c", s=2)
        yb = region(1)[:, 2048:3072].rearrange("p (s c) -> p s c", s=2)
        gated = region(1)[:, 3072:3584].rearrange("p (s n) -> p s n", s=2)
        y_got = region(1).rearrange("p (s c) -> p s c", s=4)
        xgT = region(2)[:, 0:1024].rearrange("p (s k t) -> p s k t", s=2, k=NK)
        hT = region(2)[:, 1024:1536].rearrange("p (s i q t) -> p s i q t", s=2, i=2, q=2)
        silu_h = region(2)[:, 1536:2048].rearrange("p (s n) -> p s n", s=2)
        zero_rows = region(11)[:, 0:1024]
        router_at = [2 * U + 2048]

        def scratch(*shape):
            n = 1
            for x in shape:
                n *= x
            a = router_at[0]
            router_at[0] += n
            assert router_at[0] <= 3 * U
            v = arena[:, a:a + n]
            return v if len(shape) == 1 else v.rearrange(
                "p (a b) -> p a b" if len(shape) == 2 else "p (a b c) -> p a b c",
                **dict(zip("abc", shape)))

        router_w = state[:, :, :].rearrange("p m n -> p (m n)")[:, 0:576].rearrange("p (l k n) -> p l k n", l=2, k=NK)
        router_b = state[:, :, :].rearrange("p m n -> p (m n)")[:, 576:648].rearrange("p (l n) -> p l n", l=2)
        logits, grp4, expert_m = scratch(NJ, 36), scratch(NJ, 4), scratch(NJ, 32)
        cand4, cand32, taken, two_hot = scratch(NJ, 4), scratch(NJ, 32), scratch(NJ, 32), scratch(NJ, 32)
        hot1, hot2, position = scratch(NJ, 32), scratch(NJ, 32), scratch(NJ, 32)
        g_max, g_sum, g_w, top1, top2, e21 = (scratch(NJ) for _ in range(6))
        count, blocks_e, over_before, over_upto = (scratch(32) for _ in range(4))
        passes = scratch(32, 7)
        picked = scratch(3, NJ, 2)
        pick_prod = scratch(NJ, 32)
        level8, level = scratch(NJ * 2, 7), scratch(NJ * 2)
        row_in, block_of, is_over, slot_f = (scratch(NJ * 2) for _ in range(4))
        over_cmp = region(2)[:, 0:32 * OVER].rearrange("p (b e) -> p b e", b=OVER)
        over_expert = region(2)[:, 512:528]
        over_ids, over_count = ints[:, 120:136], ints[0:1, 136:137]
        over_rows_i = ints[0:CAP, 137:138]
        combine_w = small[:, 88:96].rearrange("p (j c) -> p j c", c=2)
        slot_i = ints[:, 0:8].rearrange("p (j c) -> p j c", c=2)
        entry_i = ints[:, 8:16].rearrange("p (j c) -> p j c", c=2)
        token_i = ints[:, 16:20]
        zero_i = ints[0:CAP, 20:20 + E + OVER]
        rows_i = ints[0:CAP, 72:72 + E + OVER]
        x_rows = [nc.dram_tensor(f"x_rows{l}", (T, D), FP32, kind="Internal").ap() for l in range(2)]
        y_rows = [nc.dram_tensor(f"y_rows{l}", (SLOTS, D), FP32, kind="Internal").ap() for l in range(2)]
        table = [nc.dram_tensor(f"token_table{l}", (SLOTS, 1), I32, kind="Internal").ap() for l in range(2)]
        xT_kv = region(2).rearrange("p (k t) -> p k t", k=NK)
        xT_b = region(3).rearrange("p (k t) -> p k t", k=NK)
        w_kv = arena[:, 7 * U:10 * U].rearrange("p (k n) -> p k n", k=NK)
        w_q = arena[:, 10 * U:12 * U].rearrange("p (k n) -> p k n", k=NK)
        keys = [region(i)[:, o:o + 2048].rearrange("p (g t) -> p g t", g=NG)
                for i, o in ((1, 0), (1, 2048), (4, 0), (4, 2048))]
        values = region(5)[:, 0:2048].rearrange("p (j b n) -> p j b n", j=NJ, b=2)
        kcmp_T = region(5)[:, 2048:2172].rearrange("p (g k) -> p g k", g=NG)
        w_gate = region(5)[:, 2304:2688].rearrange("p (k n) -> p k n", k=NK)
        gates = region(5)[:, 2688:2880].rearrange("p (j n) -> p j n", j=NJ)
        NOFF = 55
        bias_c = region(5)[:, 2880:2880 + NH * NOFF].rearrange("p (h m) -> p h m", h=NH)
        fwd, rev = region(6)[0:33, 0:1024], region(6)[0:33, 1024:1664]
        rel = region(6)[0:33, 1664:1680]
        rev_rows = region(6)[0:NH, 1680:2320]
        q_T = region(6).rearrange("p (m t) -> p m t", m=NP)
        cmp_w1 = [region(i).rearrange("p (m n) -> p m n", m=16) for i in (7, 8)]
        blocks_in = [region(9)[:, o:o + 1984].rearrange("p (m g k) -> p m g k", m=16, g=NG) for o in (0, 2048)]
        cmp_w2 = [small[:, 96:352].rearrange("p (s n) -> p s n", s=2), region(5)[:, 3760:3888].rearrange("p (s n) -> p s n", s=2)]
        cmp_pe = [state[:, :, :].rearrange("p m n -> p (m n)")[:, 648 + 64 * i:712 + 64 * i].rearrange("p (m g) -> p m g", m=16) for i in range(2)]
        cmp_h = [region(11)[:, 256 * i:256 * i + 256].rearrange("p (s n) -> p s n", s=2) for i in range(2)]
        vcmp_diag = region(11)[:, 1024:2048].rearrange("p (g n) -> p g n", g=NG)
        o_rows = region(10).rearrange("p (j c) -> p j c", j=NJ)
        o_T = region(11).rearrange("p (m t) -> p m t", m=NP)
        w_o = arena[:, 7 * U:9 * U].rearrange("p (m n) -> p m n", m=NP)
        bias_h = region(2)[:, 0:2048].rearrange("p (s n) -> p s n", s=4)
        probs_T = region(2)[:, 2048:4096].rearrange("p (s b n) -> p s b n", s=2, b=2)
        cprobs_T = region(2)[:, 2048:4096].rearrange("p (s n) -> p s n", s=16)
        probs = region(3)[:, 0:3072].rearrange("p (s b n) -> p s b n", s=3, b=2)
        cprobs = region(3)[:, 3072:4096].rearrange("p (s h k) -> p s h k", s=2, h=NH)
        cmask = small[:, 352:352 + NOFF]
        cmax, csum = small[:, 408:424], small[:, 424:440]
        top, total, share = (small[:, 440 + 8 * i:446 + 8 * i].rearrange("p (s b) -> p s b", b=2) for i in range(3))
        rev_dram = nc.dram_tensor("rev_bias", (NH, P, 640), FP32, kind="Internal").ap()
        ITEMS = [(hh, j) for hh in range(NH) for j in range(NJ)]
        final_gain = region(2)[:, 0:D]
        block = stack.enter_context(nc.Block())

        @block.sync
        def _(sp):
            sp.dma_start(h, d["x"].rearrange("(j p) c -> p j c", p=P)).then_inc(sem("x_in"), 16)
            sp.dma_start(const[:, :], d["consts"]).then_inc(sem("const_in"), 16)
            sp.dma_start(vec[:, :], d["vecs"]).then_inc(sem("vec_in"), 16)
            sp.dma_start(w1l, d["a_w1"].rearrange("(p k) n -> p k n", k=NK)).then_inc(sem("lora1_in"), 16)
            sp.dma_start(a1l, d["a_a1"].rearrange("(p k) n -> p k n", k=NK)).then_inc(sem("lora1_in"), 16)
            sp.dma_start(g1l, d["a_g1"].rearrange("(p k) n -> p k n", k=NK)).then_inc(sem("lora1_in"), 16)
            sp.dma_start(w2l[0:64, :], d["a_w2"]).then_inc(sem("lora2_in"), 16)
            sp.dma_start(a2l[0:64, :], d["a_a2"]).then_inc(sem("lora2_in"), 16)
            sp.dma_start(g2l[:, :], d["a_g2"][0:128, :]).then_inc(sem("lora2_in"), 16)
            sp.dma_start(g2r[0:32, :], d["a_g2"][128:160, :]).then_inc(sem("lora2_in"), 16)
            sp.wait_ge(sem("zero_rows"), 1)
            for l in range(2):
                sp.dma_start(y_rows[l][E * CAP:SLOTS, :].rearrange("(p q) c -> p q c", p=OVER * 8),
                             spread(zero_rows[0:OVER * 8, :], 1, CAP // 8)).then_inc(sem("y_clear"), 16)
            for i, w in enumerate(("a_wk", "a_wv", "a_wr")):
                rows = d[w].rearrange("(p k) n -> k p n", k=NK)
                for k in range(NK):
                    q = 8 * i + k
                    if q >= 4:
                        sp.wait_ge(sem("mix_used"), 24 + q - 3)
                    sp.dma_start(wring[:, q % 4, :], rows[k, :, :]).then_inc(sem(f"wring{q % 4}"), 16)
            sp.wait_ge(sem("pe_s"), PACKS)
            sp.wait_ge(sem("ev_s"), PACKS)
            for m in range(NP):
                q = 24 + m
                if m >= 4:
                    sp.wait_ge(sem("wo_used"), m - 3)
                sp.dma_start(wring[:, q % 4, :], wo_rows[m, :, :]).then_inc(sem(f"wring{q % 4}"), 16)
            sp.dma_start(router_w, d["router_w"].rearrange("l (p k) n -> p l k n", k=NK)).then_inc(sem("router_in"), 16)
            sp.dma_start(router_b, d["router_b"].rearrange("l p n -> p l n")).then_inc(sem("router_in"), 16)
            sp.wait_ge(sem("table_zero"), 1)
            for l in range(2):
                sp.dma_start(table[l].rearrange("(p b) o -> p (b o)", p=CAP), zero_i).then_inc(sem("table_clear"), 16)

            def moe_loads(l):
                for e in range(E):
                    n = E * l + e
                    if e == 1:
                        for j in range(NJ):
                            sp.wait_ge(sem("xn_ready"), 4 * (1 + 2 * l) + j + 1)
                            sp.dma_start(x_rows[l][P * j:P * j + P, :], xn_m[:, j, :]).then_inc(sem("x_rows_out"), 16)
                    s = w_slot[n % 3]
                    if e == 2:
                        sp.wait_ge(sem("table_out"), 128 * (l + 1))
                        sp.dma_start(rows_i, table[l].rearrange("(p b) o -> p (b o)", p=CAP)).then_inc(sem("rows_in"), 16)
                        sp.wait_ge(sem("gather0"), 16 * (E // 2 * l + 1))
                        sp.wait_ge(sem("gather1"), 16 * (E // 2 * l + 1))
                    for i, (w, shape) in enumerate((("m_w1", "k"), ("m_w3", "k"), ("m_w2", "m"))):
                        if l == 0 and e == 0:
                            pass
                        elif l == 0 and e == 1:
                            sp.wait_ge(sem("y_ready"), NP)
                        elif l == 0 and e == 2:
                            sp.wait_ge(sem("wo_mm"), 8)
                        elif l == 1 and e == 0:
                            sp.wait_ge(sem("o_added"), at("o_added", len(ITEMS)))
                        elif l == 1 and e < 3:
                            sp.wait_ge(sem("h_nsa"), 8)
                        else:
                            sp.wait_ge(sem("hidden_mm" if i < 2 else "expert_mm"), n - 2)
                        src = d[w][l, e, :, :]
                        if shape == "k":
                            sp.dma_start(s[i].rearrange("p (k n) -> p k n", k=NK),
                                         src.rearrange("(p k) n -> p k n", k=NK)).then_inc(sem(f"w{i}_in{n % 3}"), 16)
                        else:
                            sp.dma_start(s[i].rearrange("p (k n) -> p k n", k=4),
                                         src.rearrange("(k p) n -> p k n", p=P)).then_inc(sem(f"w{i}_in{n % 3}"), 16)

            def overflow_sp(l):
                sp.wait_ge(sem("entries_ready"), l + 1)
                n_over = sp.value_load(over_count, min_val=0, max_val=OVER)
                with sp.If(n_over > 0):
                    sp.wait_ge(sem("expert_mm"), E * (l + 1))
                    with sp.Fori(0, n_over) as b:
                        e = sp.value_load(over_ids[0:1, bass.ds(b, 1)], min_val=0, max_val=E - 1)
                        for i, w in enumerate(("m_w1", "m_w3", "m_w2")):
                            src = d[w][l, bass.ds(e, 1), :, :].rearrange("o a n -> (o a) n")
                            dst = w_slot[1][i].rearrange("p (k n) -> p k n", k=NK if i < 2 else 4)
                            src = src.rearrange("(p k) n -> p k n", k=NK) if i < 2 else src.rearrange("(k p) n -> p k n", p=P)
                            sp.dma_start(dst, src).then_inc(sem(f"over_w{l}"), 16)
                        sp.wait_ge(sem(f"over_dve{l}"), 4 * b + 4)
                        for q in range(2):
                            sp.dma_start(y_rows[l][bass.ds(CAP * b + CAP * E, CAP), 512 * q:512 * q + 512],
                                         yb[CAP * q:CAP * q + CAP, 0, :]).then_inc(sem(f"over_store{l}"), 16)

            moe_loads(0)
            sp.wait_ge(sem("expert_mm"), E - 1)
            sp.dma_start(w_kv, d["kv_w"].rearrange("(p k) n -> p k n", k=NK)).then_inc(sem("kv_w_in"), 16)
            overflow_sp(0)
            sp.wait_ge(sem("combined"), 8)
            sp.dma_start(w_q, d["b_wqg"].rearrange("(p k) n -> p k n", k=NK)[:, :, 0:1024]).then_inc(sem("q_w_in"), 16)
            sp.dma_start(w_gate, d["b_wqg"].rearrange("(p k) n -> p k n", k=NK)[:, :, 1024:1072]).then_inc(sem("gate_w_in"), 16)
            sp.dma_start(fwd, d["bucket_fwd"]).then_inc(sem("bias_in"), 16)
            sp.dma_start(rev, d["bucket_rev"]).then_inc(sem("bias_in"), 16)
            sp.dma_start(rel[0:32, :], d["rel_bias"]).then_inc(sem("bias_in"), 16)
            sp.dma_start(cmp_w2[0], d["cmp_k_w2x2"].rearrange("(s p) n -> p s n", p=P)).then_inc(sem("cmp_w2_in"), 16)
            sp.dma_start(cmp_w2[1], d["cmp_v_w2"].rearrange("(s p) n -> p s n", p=P)).then_inc(sem("cmp_w2_in"), 16)
            for i in range(2):
                sp.dma_start(cmp_pe[i], d["pe_k" if i == 0 else "pe_v"]).then_inc(sem("cmp_pe_in"), 16)
            sp.wait_ge(sem("rev_ev"), at("rev_ev", 1))
            sp.dma_start(rev_dram, spread(rev_rows, 1, P)).then_inc(sem("rev_out"), 16)
            for i in range(4):
                sp.wait_ge(sem("kv_act"), at("kv_act", i + 1))
                sp.wait_ge(sem("kv_dve"), at("kv_dve", i + 1))
                sp.dma_start(keys[i][64:128, 0::2, :], keys[i][0:64, 0::2, :]).then_inc(sem("keys_in"), 16)
                sp.dma_start(keys[i][0:64, 1::2, :], keys[i][64:128, 1::2, :]).then_inc(sem("keys_in"), 16)
            sp.wait_ge(sem("kv_mm"), at("kv_mm", 12))
            for i in range(2):
                sp.dma_start(cmp_w1[i], d["cmp_k_w1" if i == 0 else "cmp_v_w1"].rearrange(
                    "(m p) n -> p m n", p=P)).then_inc(sem("cmp_w1_in"), 16)

            def load_bias(hh):
                sp.dma_start(bias_h[:, hh % 4, :], bass.AP(tensor=rev_dram.tensor, offset=640 * P * hh + 127,
                                                           ap=[[639, P], [1, 512]])).then_inc(sem(f"bias_h{hh % 4}"), 16)

            sp.wait_ge(sem("rev_out"), 16)
            for hh in range(4):
                load_bias(hh)
            sp.wait_ge(sem("cmp_hidden"), at("cmp_hidden", 2))
            sp.dma_start(w_o, d["b_wo"].rearrange("(m p) n -> p m n", p=P)).then_inc(sem("b_wo_in"), 16)
            for hh in range(4, NH):
                sp.wait_ge(sem("biased"), at("biased", 4 * (hh - 3)))
                load_bias(hh)
            moe_loads(1)
            overflow_sp(1)
            sp.wait_ge(sem("combined"), 16)
            sp.dma_start(final_gain, d["final_ln"].rearrange("(o c) -> o c", o=1).broadcast_to([P, D])).then_inc(sem("final_in"), 16)
            for j in range(NJ):
                sp.wait_ge(sem("out_ready"), j + 1)
                sp.dma_start(out[P * j:P * j + P, :], xn_m[:, j, :]).then_inc(sem("out_done"), 16)
            sp.wait_ge(sem("out_done"), 64)

        @block.gpsimd
        def _(pool):
            nc.gpsimd.memset(zero_rows, 0.0).then_inc(sem("zero_rows"), 1)
            pool.wait_ge(sem("const_in"), 16)
            nc.gpsimd.memset(state[:, :, :], 0.0).then_inc(sem("state_zero"), 1)
            mask = cst("head_mask").rearrange("p (a t) -> p a t", a=2)

            def expand(dst, src, m, c):
                nc_op = nc.gpsimd.tensor_tensor(dst.rearrange("p (a t) -> p a t", a=2),
                                                spread(src[:, m, c * C:c * C + C], 1, 2), mask, ALU.mult)
                return nc_op

            for m in range(NP):
                pool.wait_ge(sem("operands_act"), m + 1)
                pool.wait_ge(sem("rk_ready"), m + 1)
                nc.gpsimd.tensor_tensor(b_T[:, m, :], b_T[:, m, :], tmp[:, 2, m % 2, :], ALU.mult)
                nc.gpsimd.tensor_tensor(k_T[:, m, :], k_T[:, m, :], tmp[:, 2, m % 2, :],
                                        ALU.mult).then_inc(sem("operands_pool"), 1)

            pool.wait_ge(sem("operands_dve"), NP)
            pool.wait_ge(sem("operands_pool"), NP)
            pool.wait_ge(sem("bonus_ev"), NP)
            for tick in range(-1, PACKS + 11):
                own, given = last_of(tick, [("ex_ab", -1), ("ex_late", 6), ("ev_x0", 0), ("s_decayed", 9)])
                if own:
                    pool.wait_ge(sem(own), given)
                n = tick + 1
                if n < PACKS:
                    if n >= 2:
                        pool.wait_ge(sem("pe_g"), n - 1)
                    expand(ab_e[:, n % 2, 0:128], a_T, n % NP, n // NP)
                    expand(ab_e[:, n % 2, 128:256], b_T, n % NP, n // NP).then_inc(sem("ex_ab"), 1)
                n = tick - 6
                if 0 <= n < PACKS:
                    if n >= 2:
                        pool.wait_ge(sem("pe_tr"), n - 1)
                    if n >= 4:
                        pool.wait_ge(sem("pe_rh"), n - 3)
                    for i, src in enumerate((b_T, k_T, v_T)):
                        expand(bkv_e[:, n % 2, 128 * i:128 * i + 128], src, n % NP, n // NP)
                    expand(a_e[:, n % 4, :], a_T, n % NP, n // NP).then_inc(sem("ex_late"), 1)
                n = tick
                if 0 <= n < PACKS:
                    pool.wait_ge(sem("ev_g"), n + 1)
                    if n >= 2:
                        pool.wait_ge(sem("pe_l1"), n - 1)
                        pool.wait_ge(sem("ev_x1"), n - 1)
                    nc.gpsimd.tensor_tensor(lv[1][:, n % 2, 0:128], at32[:, n % 2, :], ident,
                                            ALU.add).then_inc(sem("ev_x0"), 1)
                n = tick - 9
                if 0 <= n < PACKS:
                    m, c = n % NP, n // NP
                    if c == 0:
                        pool.wait_ge(sem("state_zero"), 1)
                    else:
                        pool.wait_ge(sem("ev_s"), n - NP + 1)
                    if n >= 2:
                        pool.wait_ge(sem("ev_s"), n - 1)
                    nc.gpsimd.tensor_scalar(s_dec[:, n % 2, :], state[:, m, :], chunk_decay[:, m, c:c + 1], None,
                                            ALU.mult).then_inc(sem("s_decayed"), 1)
            nc.gpsimd.memset(zero_i, 0).then_inc(sem("table_zero"), 1)

            def moe_pool(l):
                pool.wait_ge(sem("table_clear"), 32)
                pool.wait_ge(sem("entries_ready"), l + 1)
                for j in range(NJ):
                    for c in range(2):
                        nc.gpsimd.indirect_dma_start(
                            out=table[l], out_offset=bass.IndirectOffsetOnAxis(ap=entry_i[:, j, c:c + 1], axis=0),
                            in_=token_i[:, j:j + 1], in_offset=None).then_inc(sem("table_out"), 16)
                pool.wait_ge(sem("x_rows_out"), 64 * (l + 1))
                pool.wait_ge(sem("rows_in"), 16 * (l + 1))
                for e in range(E):
                    n = E * l + e
                    if e >= 2:
                        pool.wait_ge(sem("gathered_T"), n - 1)
                    nc.gpsimd.indirect_dma_start(
                        out=xg[:, n % 2, :], out_offset=None, in_=x_rows[l],
                        in_offset=bass.IndirectOffsetOnAxis(ap=rows_i[:, e:e + 1], axis=0)
                    ).then_inc(sem(f"gather{n % 2}"), 16)
                n_over = pool.value_load(over_count, min_val=0, max_val=OVER)
                with pool.If(n_over > 0):
                    pool.wait_ge(sem("expert_mm"), E * (l + 1))
                    with pool.Fori(0, n_over) as b:
                        nc.gpsimd.tensor_copy(over_rows_i, rows_i[:, bass.ds(b + E, 1)]).then_inc(sem(f"over_row_ids{l}"), 1)
                        pool.wait_ge(sem(f"over_row_ids{l}"), b + 1)
                        pool.sem_inc(sem("over_turn_pool"), 1)
                        nc.gpsimd.indirect_dma_start(
                            out=xg[:, 0, :], out_offset=None, in_=x_rows[l],
                            in_offset=bass.IndirectOffsetOnAxis(ap=over_rows_i, axis=0)).then_inc(sem(f"over_x{l}"), 16)
                        pool.wait_ge(sem(f"over_pe{l}"), 4 * b + 1)
                        pool.wait_ge(sem(f"over_store{l}"), 32 * b + 32)
                pool.wait_ge(sem("y_store0"), 32 * 16 * (l + 1))
                pool.wait_ge(sem("y_store1"), 32 * 16 * (l + 1))
                for j in range(NJ):
                    for c in range(2):
                        q = 2 * j + c
                        if q >= 4:
                            pool.wait_ge(sem("combined"), 8 * l + q - 3)
                        nc.gpsimd.indirect_dma_start(
                            out=y_got[:, q % 4, :], out_offset=None, in_=y_rows[l],
                            in_offset=bass.IndirectOffsetOnAxis(ap=slot_i[:, j, c:c + 1], axis=0)
                        ).then_inc(sem(f"y_got{q % 4}"), 16)

            moe_pool(0)
            pool.wait_ge(sem("kv_mm"), at("kv_mm", 12))
            pool.wait_ge(sem("q_mm"), at("q_mm", 1))
            pool.wait_ge(sem("gate_mm"), at("gate_mm", 1))
            nc.gpsimd.memset(vcmp_diag, 0.0)
            nc.gpsimd.memset(cprobs, 0.0).then_inc(sem("cmp_zero"), 1)
            moe_pool(1)

        @block.scalar
        def _(act):
            def norm_squares(i, xn):
                for j in range(NJ):
                    last = nc.scalar.activation(xn[:, j, :], h[:, j, :], ACT.Square, accum_out=sumsq[:, j:j + 1])
                last.then_inc(sem("norm_sq"), 1)
                act.wait_ge(sem("norm_var"), i + 1)
                nc.scalar.activation(rstd, sumsq, ACT.Sqrt).then_inc(sem("norm_std"), 1)

            def norm_evacuate(i, dst, gain):
                for k in range(0, NK, 2):
                    act.wait_ge(sem("tr_done"), 8 * i + k + 1)
                    nc.scalar.activation(dst[:, k, :], bank[k][:, :], ACT.Copy,
                                         scale=gain[:, k:k + 1]).then_inc(sem("xT_act"), 1)

            act.wait_ge(sem("x_in"), 16)
            norm_squares(0, xn)
            act.wait_ge(sem("vec_in"), 16)
            norm_evacuate(0, xT, v8("a_ln"))

            act.wait_ge(sem("lora_hid"), 1)
            nc.scalar.activation(hid_w[0:64, :], bank[0][0:64, :], ACT.Tanh).then_inc(sem("hid_ev"), 1)
            act.wait_ge(sem("lora_hid"), 2)
            nc.scalar.activation(hid_a[0:64, :], bank[1][0:64, :], ACT.Copy).then_inc(sem("hid_ev"), 1)
            act.wait_ge(sem("lora_hid"), 3)
            nc.scalar.activation(hid_g[:, :], bank[2][:, :], ACT.Sigmoid)
            nc.scalar.activation(hid_r[0:32, :], bank[3][0:32, :], ACT.Sigmoid).then_inc(sem("hid_ev"), 1)
            for m in range(NP):
                act.wait_ge(sem("lora_mm"), 3 * m + 1)
                if m >= 2:
                    act.wait_ge(sem("scan_done"), m - 1)
                nc.scalar.activation(sig[:, m % 2, :], bank[4 + (3 * m) % 4][:, :], ACT.Sigmoid,
                                     bias=v8("w0")[:, m:m + 1]).then_inc(sem("lora_ev"), 1)
                act.wait_ge(sem("lora_mm"), 3 * m + 2)
                nc.scalar.activation(b_T[:, m, :], bank[4 + (3 * m + 1) % 4][:, :], ACT.Sigmoid,
                                     bias=v8("a0")[:, m:m + 1]).then_inc(sem("lora_ev"), 1)
                act.wait_ge(sem("lora_mm"), 3 * m + 3)
                nc.scalar.activation(g_T[:, m, :], bank[4 + (3 * m + 2) % 4][:, :],
                                     ACT.Copy).then_inc(sem("lora_ev"), 1)
            for i, dst in enumerate((k_T, v_T, r_T)):
                for m in range(NP):
                    act.wait_ge(sem("proj_mm"), 8 * i + m + 1)
                    if i == 1 and m == 0:
                        act.wait_ge(sem("scan_done"), NP)
                    nc.scalar.activation(dst[:, m, :], bank[m][:, :], ACT.Copy).then_inc(sem("proj_ev"), 1)
                if i == 0:
                    act.wait_ge(sem("proj_ev"), 8)
                    for m in range(NP):
                        nc.scalar.activation(a_T[:, m, :], k_T[:, m, :], ACT.Square,
                                             scale=v8("kk")[:, m:m + 1]).then_inc(sem("k_sq"), 1)
                if i == 1:
                    for m in range(NP):
                        act.wait_ge(sem("k_norm2"), m + 1)
                        nc.scalar.activation(a_T[:, m, :], a_T[:, m, :], ACT.Sqrt).then_inc(sem("k_norm"), 1)
                    act.wait_ge(sem("mix_ready"), 48)
                    act.wait_ge(sem("one_ka"), 1)
                    for m in range(NP):
                        if m >= 2:
                            act.wait_ge(sem("k_scaled"), m - 1)
                        nc.scalar.activation(tmp[:, 0, m % 2, :], b_T[:, m, :], ACT.Identity,
                                             scale=v8("ka")[:, m:m + 1],
                                             bias=one_ka[:, m:m + 1]).then_inc(sem("k_factor"), 1)
            act.wait_ge(sem("scan_done"), NP)
            for m in range(NP):
                if m >= 2:
                    act.wait_ge(sem("operands_dve"), m - 1)
                    act.wait_ge(sem("operands_pool"), m - 1)
                nc.scalar.activation(tmp[:, 1, m % 2, :], l_T[:, m, :], ACT.Exp, scale=-DECAY)
                nc.scalar.activation(tmp[:, 2, m % 2, :], l_T[:, m, :], ACT.Exp, scale=DECAY)
                nc.scalar.activation(chunk_decay[:, m, :], l_T[:, m, C - 1::C], ACT.Exp,
                                     scale=-DECAY).then_inc(sem("operands_act"), 1)

            for tick in range(PACKS + 11):
                own, given = last_of(tick, [("ev_sq", 1), ("ev_l1", 2), ("ev_l2", 3), ("ev_l3", 4), ("ev_mz", 6), ("ev_rh", 8),
                                     ("ev_y", 10), ("ev_tr", 7)])
                if own:
                    act.wait_ge(sem(own), given)
                for off, name, src, dst in (
                        (1, "sq", p_sq, lambda n: lv[1][:, n % 2, 128:384]),
                        (2, "l1", p_l1[:, 128:384], lambda n: lv[2][:, n % 2, 128:384]),
                        (3, "l2", p_l2[:, 128:384], lambda n: lv[3][:, n % 2, 128:384]),
                        (4, "l3", p_l3[:, 128:256], lambda n: lv[4][:, n % 2, 128:256]),
                        (6, "mz", p_mz, lambda n: tz[:, n % 2, :]),
                        (8, "rh", p_rh, lambda n: rhs_s[:, n % 2, :]),
                        (10, "y", p_y, lambda n: y_T[:, n % NP, (n // NP) * C:(n // NP) * C + C]),
                        (7, "tr", p_tr, lambda n: bkv_s[:, n % 4, :])):
                    n = tick - off
                    if 0 <= n < PACKS:
                        act.wait_ge(sem("ev_x" + name[1] if name in ("l1", "l2", "l3") else "pe_" + name), n + 1)
                        nc.scalar.activation(dst(n), src, ACT.Copy).then_inc(sem("ev_" + name), 1)

            for m in range(NP):
                act.wait_ge(sem("y_centered"), m + 1)
                nc.scalar.activation(r_T[:, m, :], y_T[:, m, :], ACT.Square).then_inc(sem("y_sq"), 1)
                if m >= 1:
                    act.wait_ge(sem("y_var"), m)
                    nc.scalar.activation(a_T[:, m - 1, :], a_T[:, m - 1, :], ACT.Sqrt).then_inc(sem("y_std"), 1)
            act.wait_ge(sem("y_var"), NP)
            nc.scalar.activation(a_T[:, NP - 1, :], a_T[:, NP - 1, :], ACT.Sqrt).then_inc(sem("y_std"), 1)
            def moe_act(l):
                i = 1 + 2 * l
                norm_squares(i, xn_m)
                norm_evacuate(i, xT_m, v8(f"m_ln{l}"))
                act.wait_ge(sem("group_shifted"), l + 1)
                nc.scalar.activation(grp4, grp4, ACT.Exp).then_inc(sem("group_exp"), 1)
                act.wait_ge(sem("top_diff"), l + 1)
                nc.scalar.activation(e21, e21, ACT.Exp).then_inc(sem("top_exp"), 1)
                for e in range(E):
                    n = E * l + e
                    act.wait_ge(sem("hidden_mm"), n + 1)
                    if n >= 2:
                        act.wait_ge(sem("gated_ready"), n - 1)
                    nc.scalar.activation(silu_h[:, n % 2, :], bank[4 + n % 2][:, 0:256], ACT.Silu).then_inc(sem("silu"), 1)
                    act.wait_ge(sem("expert_mm"), n + 1)
                    if e >= 2:
                        act.wait_ge(sem(f"y_store{n % 2}"), 32 * (n // 2))
                    nc.scalar.activation(yb[:, n % 2, :], bank[6 + n % 2][:, :], ACT.Copy).then_inc(sem("yb_ready"), 1)
                    act.wait_ge(sem("yb_ready"), n + 1)
                    for q in range(2):
                        act.dma_start(y_rows[l][CAP * e:CAP * e + CAP, 512 * q:512 * q + 512],
                                      yb[CAP * q:CAP * q + CAP, n % 2, :]).then_inc(sem(f"y_store{n % 2}"), 16)
                n_over = act.value_load(over_count, min_val=0, max_val=OVER)
                with act.If(n_over > 0):
                    with act.Fori(0, n_over) as b:
                        act.wait_ge(sem(f"over_pe{l}"), 4 * b + 2)
                        nc.scalar.activation(silu_h[:, 0, :], bank[4][:, 0:256], ACT.Silu).then_inc(sem(f"over_act{l}"), 1)
                        act.wait_ge(sem(f"over_dve{l}"), 4 * b + 2)

            act.wait_ge(sem("h_rwkv"), 8)
            moe_act(0)
            link_a = [0]

            def then_a(ins):
                link_a[0] += 1
                ins.then_inc(sem("act_link"), 1)
                act.wait_ge(sem("act_link"), link_a[0])

            act.wait_ge(sem("combined"), 8)
            norm_squares(2, xn_m)
            for k in range(0, NK, 2):
                act.wait_ge(sem("tr_done"), 16 + k + 1)
                nc.scalar.activation(xT_kv[:, k, :], bank[k][:, :], ACT.Copy, scale=v8("kv_ln")[:, k:k + 1])
                nc.scalar.activation(xT_b[:, k, :], bank[k][:, :], ACT.Copy, scale=v8("b_ln")[:, k:k + 1]).then_inc(sem("xT_act"), 1)
            act.wait_ge(sem("tr_done"), 24)
            for u in range(0, 12, 2):
                act.wait_ge(sem("kv_mm"), at("kv_mm", u + 1))
                b = bank[u % 8]
                if u < 8:
                    kind, gt = u // 2, u % 2
                    nc.scalar.activation(keys[kind][0:64, 0, :], b[0:64, :], ACT.Copy)
                    nc.scalar.activation(keys[kind][64:128, 1, :], b[64:128, :], ACT.Copy).then_inc(sem("kv_act"), 1)
                else:
                    nc.scalar.activation(values[:, u - 8, :, :], b[:, :].rearrange("p (b n) -> p b n", b=2),
                                         ACT.Copy).then_inc(sem("kv_act"), 1)
            act.wait_ge(sem("bias_mm"), at("bias_mm", 1))
            nc.scalar.activation(bias_c[:, :, 0:32], bank[4][:, :].rearrange("p (m h) -> p h m", h=NH), ACT.Copy)
            nc.scalar.activation(bias_c[:, :, 32:NOFF], bank[5][:, 0:16 * (NOFF - 32)].rearrange("p (m h) -> p h m", h=NH), ACT.Copy)
            nc.scalar.activation(rev_rows[:, 0:512], bank[6][0:NH, :], ACT.Copy)
            nc.scalar.activation(rev_rows[:, 512:640], bank[7][0:NH, 0:128], ACT.Copy).then_inc(sem("rev_ev"), 1)
            act.wait_ge(sem("rev_out"), 16)
            for m in range(0, NP, 2):
                act.wait_ge(sem("q_mm"), at("q_mm", m + 1))
                nc.scalar.activation(q_T[:, m, :], bank[m][:, :], ACT.Copy, scale=HD ** -0.5).then_inc(sem("q_act"), 1)
            act.wait_ge(sem("gate_mm"), at("gate_mm", 1))
            nc.scalar.activation(gates, bank[0][:, 0:256].rearrange("p (j n) -> p j n", j=NJ)[:, :, 0:48],
                                 ACT.Sigmoid).then_inc(sem("gates_ready"), 1)
            for i in range(2):
                act.wait_ge(sem("cmp_hidden"), at("cmp_hidden", i + 1))
                nc.scalar.activation(cmp_h[i][:, :, 0:124], bank[2 + i][:, 0:256].rearrange("p (s n) -> p s n", s=2)[:, :, 0:124],
                                     ACT.Gelu_apprx_tanh).then_inc(sem("cmp_act"), 1)
            act.wait_ge(sem("cmp_out"), at("cmp_out", 1))
            nc.scalar.activation(kcmp_T, bank[4][:, 0:124].rearrange("p (g k) -> p g k", g=NG), ACT.Copy).then_inc(sem("kcmp_ready"), 1)
            for j in range(NJ):
                act.wait_ge(sem("cshifted"), at("cshifted", j + 1))
                nc.scalar.activation(cprobs[:, j % 2, :, 0:NCMP], cprobs[:, j % 2, :, 0:NCMP], ACT.Exp).then_inc(sem("cexp"), 1)
                act.wait_ge(sem("cT_mm"), at("cT_mm", j + 1))
                if j == 0:
                    act.wait_ge(sem("kv_mm"), at("kv_mm", 12))
                nc.scalar.activation(cprobs_T[:, 4 * j:4 * j + 4, :], bank[6][:, :].rearrange("p (g t) -> p g t", g=NG),
                                     ACT.Copy).then_inc(sem("cT_ready"), 1)
            for tick in range(len(ITEMS) + 2):
                n = tick - 2
                if n >= 0:
                    hh, j = ITEMS[n]
                    act.wait_ge(sem("probs_mm"), at("probs_mm", n + 1))
                    nc.scalar.activation(probs_T[:, n % 2, 0, 0:P * (j + 1)], bank[4][:, 0:P * (j + 1)],
                                         ACT.Copy).then_inc(sem("pT_act"), 1)
                n = tick
                if n < len(ITEMS):
                    hh, j = ITEMS[n]
                    act.wait_ge(sem("biased"), at("biased", n + 1))
                    for b in range(2):
                        last = nc.scalar.activation(probs[:, n % 3, b, 0:P * (j + 1)], probs[:, n % 3, b, 0:P * (j + 1)],
                                                    ACT.Exp, bias=top[:, n % 3, b:b + 1], accum_out=total[:, n % 3, b:b + 1])
                    last.then_inc(sem("probs_ready"), 1)
            for m in range(0, NP, 2):
                act.wait_ge(sem("oT_mm"), at("oT_mm", m + 1))
                nc.scalar.activation(o_T[:, m, :], bank[m][:, :], ACT.Copy).then_inc(sem("oT_act"), 1)
            act.wait_ge(sem("h_nsa"), 8)
            moe_act(1)
            act.wait_ge(sem("combined"), 16)
            norm_squares(4, xn_m)

        @block.vector
        def _(dve):
            def norm_scale(i, xn):
                dve.wait_ge(sem("norm_sq"), i + 1)
                nc.vector.tensor_scalar(sumsq, sumsq, 1.0 / D, EPS, ALU.mult, ALU.add).then_inc(sem("norm_var"), 1)
                dve.wait_ge(sem("norm_std"), i + 1)
                nc.vector.reciprocal(rstd, rstd).then_inc(sem("norm_rstd"), 1)
                dve.wait_ge(sem("norm_rstd"), i + 1)
                for j in range(NJ):
                    nc.vector.tensor_scalar(xn[:, j, :], h[:, j, :], rstd[:, j:j + 1], None,
                                            ALU.mult).then_inc(sem("xn_ready"), 1)

            def norm_evacuate(i, dst, gain):
                for k in range(1, NK, 2):
                    dve.wait_ge(sem("tr_done"), 8 * i + k + 1)
                    nc.vector.tensor_scalar(dst[:, k, :], bank[k][:, :], gain[:, k:k + 1], None,
                                            ALU.mult).then_inc(sem("xT_dve"), 1)

            dve.wait_ge(sem("x_in"), 16)
            norm_scale(0, xn)
            dve.wait_ge(sem("vec_in"), 16)
            norm_evacuate(0, xT, v8("a_ln"))
            nc.vector.tensor_scalar(one_ka, v8("ka"), -1.0, 1.0, ALU.mult, ALU.add).then_inc(sem("one_ka"), 1)
            dve.wait_ge(sem("xT_act"), 4)
            dve.wait_ge(sem("xT_dve"), 4)
            nc.vector.tensor_tensor(xxT[:, :, 1:T], xT[:, :, 0:T - 1], xT[:, :, 1:T], ALU.subtract)
            nc.vector.tensor_scalar(xxT[:, :, 0:1], xT[:, :, 0:1], -1.0, None, ALU.mult).then_inc(sem("xx_ready"), 1)
            dve.wait_ge(sem("xx_ready"), 1)

            def mixes(i, mu):
                for k in range(NK):
                    q = 8 * i + k
                    if q >= 8:
                        dve.wait_ge(sem("mix_used"), q - 7)
                    nc.vector.scalar_tensor_tensor(mix[:, q % 8, :], xxT[:, k, :], v8(f"mu{mu}")[:, k:k + 1],
                                                   xT[:, k, :], ALU.mult, ALU.add).then_inc(sem("mix_ready"), 1)

            mixes(0, 1)
            mixes(1, 4)
            mixes(2, 5)
            dve.wait_ge(sem("const_in"), 16)
            dve.wait_ge(sem("y_clear"), 32)
            for m in range(2):
                dve.wait_ge(sem("lora_ev"), 3 * m + 1)
                nc.vector.tensor_tensor_scan(l_T[:, m, :], cst("scan_keep"), sig[:, m % 2, :], 0.0,
                                             ALU.mult, ALU.add).then_inc(sem("scan_done"), 1)
            mixes(3, 2)
            for m in range(2, NP):
                dve.wait_ge(sem("lora_ev"), 3 * m + 1)
                nc.vector.tensor_tensor_scan(l_T[:, m, :], cst("scan_keep"), sig[:, m % 2, :], 0.0,
                                             ALU.mult, ALU.add).then_inc(sem("scan_done"), 1)
            mixes(4, 3)
            for m in range(NP):
                dve.wait_ge(sem("k_ssq"), m + 1)
                nc.vector.tensor_scalar(a_T[:, m, :], bank[m][:, :], 1e-24, None,
                                        ALU.max).then_inc(sem("k_norm2"), 1)
            mixes(5, 0)
            for m in range(NP):
                dve.wait_ge(sem("k_norm"), m + 1)
                nc.vector.reciprocal(a_T[:, m, :], a_T[:, m, :]).then_inc(sem("k_rnorm"), 1)
                dve.wait_ge(sem("k_rnorm"), m + 1)
                nc.vector.scalar_tensor_tensor(a_T[:, m, :], k_T[:, m, :], v8("kk")[:, m:m + 1], a_T[:, m, :],
                                               ALU.mult, ALU.mult).then_inc(sem("kk_ready"), 1)
                dve.wait_ge(sem("k_factor"), m + 1)
                dve.wait_ge(sem("kk_ready"), m + 1)
                nc.vector.tensor_tensor(b_T[:, m, :], b_T[:, m, :], a_T[:, m, :], ALU.mult)
                nc.vector.tensor_tensor(k_T[:, m, :], k_T[:, m, :], tmp[:, 0, m % 2, :],
                                        ALU.mult).then_inc(sem("k_scaled"), 1)
            for m in range(NP):
                dve.wait_ge(sem("proj_ev"), 17 + m)
                dve.wait_ge(sem("operands_act"), m + 1)
                dve.wait_ge(sem("k_scaled"), m + 1)
                if m >= 2:
                    dve.wait_ge(sem("bonus_mm"), m - 1)
                nc.vector.scalar_tensor_tensor(tmp[:, 3, m % 2, :], r_T[:, m, :], v8("rk")[:, m:m + 1], k_T[:, m, :],
                                               ALU.mult, ALU.mult).then_inc(sem("rk_ready"), 1)
                dec, kk_v = (x.rearrange("p (c t) -> p c t", t=C) for x in (tmp[:, 1, m % 2, :], a_T[:, m, :]))
                nc.vector.scalar_tensor_tensor(kk_v[:, :, 1:C], kk_v[:, :, 1:C], -1.0, dec[:, :, 0:C - 1],
                                               ALU.mult, ALU.mult)
                nc.vector.tensor_scalar(kk_v[:, :, 0:1], kk_v[:, :, 0:1], -1.0, None, ALU.mult)
                dve.wait_ge(sem("rk_ready"), m + 1)
                nc.vector.tensor_tensor(r_T[:, m, :], r_T[:, m, :], tmp[:, 1, m % 2, :],
                                        ALU.mult).then_inc(sem("operands_dve"), 1)
                dve.wait_ge(sem("bonus_mm"), m + 1)
                nc.vector.tensor_tensor(l_T[:, m, :], bank[m][:, :], v_T[:, m, :], ALU.mult).then_inc(sem("bonus_ev"), 1)

            up32 = cst("upper32").rearrange("p (a t) -> p a t", a=2)
            up64 = cst("upper64").rearrange("p (a t) -> p a t", a=2)
            for tick in range(PACKS + 11):
                own, given = last_of(tick, [("ev_g", 0), ("ev_x1", 2), ("ev_x2", 3), ("ev_x3", 4), ("ev_x4", 5), ("ev_mx", 7),
                                     ("ev_u", 9), ("ev_late", 7), ("ev_s", 10)])
                if own:
                    dve.wait_ge(sem(own), given)
                n = tick
                if n < PACKS:
                    dve.wait_ge(sem("pe_g"), n + 1)
                    if n >= 2:
                        dve.wait_ge(sem("pe_sq"), n - 1)
                        dve.wait_ge(sem("ev_x0"), n - 1)
                    nc.vector.tensor_tensor(at32[:, n % 2, :].rearrange("p (a t) -> p a t", a=2),
                                            spread(p_g, 1, 2), up32, ALU.mult)
                    nc.vector.tensor_tensor(a32[:, n % 2, :], p_a, cst("lower32"), ALU.mult)
                    nc.vector.tensor_tensor(a_off[:, n % 8, :], p_a, cst("lower_off"), ALU.mult).then_inc(sem("ev_g"), 1)
                for off, name, src, add, dst in (
                        (2, "1", p_l1[:, 0:128], lambda n: lv[1][:, n % 2, 0:128], lambda n: lv[2][:, n % 2, 0:128]),
                        (3, "2", p_l2[:, 0:128], lambda n: lv[2][:, n % 2, 0:128], lambda n: lv[3][:, n % 2, 0:128]),
                        (4, "3", p_l3[:, 0:128], lambda n: lv[3][:, n % 2, 0:128], lambda n: lv[4][:, n % 2, 0:128]),
                        (5, "4", p_l4, lambda n: lv[4][:, n % 2, 0:128], lambda n: x4[:, n % 4, :])):
                    n = tick - off
                    if 0 <= n < PACKS:
                        dve.wait_ge(sem("pe_l" + name), n + 1)
                        if name != "1":
                            dve.wait_ge(sem("ev_x" + str(int(name) - 1)), n + 1)
                        nc.vector.tensor_tensor(dst(n), src, add(n), ALU.add).then_inc(sem("ev_x" + name), 1)
                n = tick - 7
                if 0 <= n < PACKS:
                    dve.wait_ge(sem("pe_mx"), n + 1)
                    nc.vector.tensor_tensor(x_all[:, n % 4, :], p_mx, x4[:, n % 4, :], ALU.add).then_inc(sem("ev_mx"), 1)
                n = tick - 9
                if 0 <= n < PACKS:
                    dve.wait_ge(sem("pe_u"), n + 1)
                    nc.vector.tensor_copy(u_s[:, n % 4, :], p_u).then_inc(sem("ev_u"), 1)
                n = tick - 7
                if 0 <= n < PACKS:
                    dve.wait_ge(sem("pe_tr"), n + 1)
                    nc.vector.tensor_tensor(ak_t[:, n % 4, :].rearrange("p (a t) -> p a t", a=2),
                                            spread(p_late[:, 128:192], 1, 2), up64, ALU.mult)
                    nc.vector.tensor_tensor(rbk[:, n % 4, :], p_late[:, 0:128], cst("upper_incl"),
                                            ALU.mult).then_inc(sem("ev_late"), 1)
                n = tick - 10
                if 0 <= n < PACKS:
                    m, c = n % NP, n // NP
                    dve.wait_ge(sem("pe_s"), n + 1)
                    dve.wait_ge(sem("s_decayed"), n + 1)
                    nc.vector.scalar_tensor_tensor(state[:, m, :], p_s, chunk_decay[:, m, c:c + 1],
                                                   s_dec[:, n % 2, :], ALU.mult, ALU.add).then_inc(sem("ev_s"), 1)

            dve.wait_ge(sem("ev_y"), PACKS)
            for m in range(NP):
                dve.wait_ge(sem("y_mean"), m + 1)
                nc.vector.scalar_tensor_tensor(y_T[:, m, :], bank[m % 4][:, :], -1.0 / HD, y_T[:, m, :], ALU.mult,
                                               ALU.add).then_inc(sem("y_centered"), 1)
            for m in range(NP):
                dve.wait_ge(sem("y_ssq"), m + 1)
                nc.vector.tensor_scalar(a_T[:, m, :], bank[4 + m % 4][:, :], 1.0 / HD, GN_EPS, ALU.mult,
                                        ALU.add).then_inc(sem("y_var"), 1)
            link = [0]

            def then(ins):
                link[0] += 1
                ins.then_inc(sem("dve_link"), 1)
                dve.wait_ge(sem("dve_link"), link[0])

            for m in range(NP):
                dve.wait_ge(sem("y_std"), m + 1)
                then(nc.vector.reciprocal(a_T[:, m, :], a_T[:, m, :]))
                then(nc.vector.scalar_tensor_tensor(y_T[:, m, :], y_T[:, m, :], v8("lnx_w")[:, m:m + 1], a_T[:, m, :],
                                                    ALU.mult, ALU.mult))
                then(nc.vector.scalar_tensor_tensor(y_T[:, m, :], y_T[:, m, :], v8("lnx_b")[:, m:m + 1], l_T[:, m, :],
                                                    ALU.add, ALU.add))
                nc.vector.tensor_tensor(y_T[:, m, :], y_T[:, m, :], g_T[:, m, :], ALU.mult).then_inc(sem("y_ready"), 1)
            for j in range(NJ):
                for q in range(2):
                    dve.wait_ge(sem("wo_mm"), 2 * j + q + 1)
                    last = nc.vector.tensor_tensor(h[:, j, 512 * q:512 * q + 512], bank[2 * j + q][:, :],
                                                   h[:, j, 512 * q:512 * q + 512], ALU.add)
                    last.then_inc(sem("h_rwkv"), 1)
            def moe_dve(l):
                i = 1 + 2 * l
                norm_scale(i, xn_m)
                norm_evacuate(i, xT_m, v8(f"m_ln{l}"))
                dve.wait_ge(sem("router_in"), 32)
                dve.wait_ge(sem("router_mm"), at("router_mm", l + 1))
                then(nc.vector.tensor_tensor(logits, bank[0][:, 0:256].rearrange("p (j n) -> p j n", j=NJ)[:, :, 0:36],
                                             spread(router_b[:, l, :], 1, NJ), ALU.add))
                iota4, iota32 = spread(cst("iota")[:, 0:4], 1, NJ), spread(cst("iota"), 1, NJ)
                groups = logits[:, :, 0:4]

                def first_largest(hot, largest, x, cand, iota, n):
                    then(nc.vector.reduce_max(largest, x, axis=AX.X))
                    then(nc.vector.tensor_tensor(hot, x, spread(largest, 2, n), ALU.is_equal))
                    then(nc.vector.scalar_tensor_tensor(cand, hot, -64.0, iota, ALU.mult, ALU.add))
                    then(nc.vector.tensor_reduce(level[:, 0:4], cand, axis=AX.X, op=ALU.min))
                    then(nc.vector.tensor_tensor(hot, cand, spread(level[:, 0:4], 2, n), ALU.is_equal))

                first_largest(two_hot[:, :, 0:4], g_max, groups, cand4, iota4, 4)
                nc.vector.tensor_tensor(grp4, groups, spread(g_max, 2, 4), ALU.subtract).then_inc(sem("group_shifted"), 1)
                then(nc.vector.tensor_scalar(cand4, two_hot[:, :, 0:4], -NEG, NEG, ALU.mult, ALU.add))
                then(nc.vector.tensor_tensor(expert_m.rearrange("p j (g e) -> p j g e", g=4),
                                             logits[:, :, 4:36].rearrange("p j (g e) -> p j g e", g=4),
                                             spread(cand4, 3, 8), ALU.add))
                first_largest(hot1, top1, expert_m, cand32, iota32, 32)
                then(nc.vector.scalar_tensor_tensor(taken, hot1, 3 * NEG, expert_m, ALU.mult, ALU.add))
                first_largest(hot2, top2, taken, cand32, iota32, 32)
                nc.vector.tensor_tensor(e21, top2, top1, ALU.subtract).then_inc(sem("top_diff"), 1)
                nc.vector.tensor_tensor(two_hot, hot1, hot2, ALU.add).then_inc(sem("two_hot"), 1)
                dve.wait_ge(sem("group_exp"), l + 1)
                then(nc.vector.reduce_sum(g_sum, grp4, axis=AX.X))
                dve.wait_ge(sem("top_exp"), l + 1)
                then(nc.vector.tensor_scalar(g_w, e21, 1.0, None, ALU.add))
                then(nc.vector.tensor_tensor(g_w, g_w, g_sum, ALU.mult))
                then(nc.vector.reciprocal(g_w, g_w))
                then(nc.vector.tensor_copy(combine_w[:, :, 0], g_w))
                then(nc.vector.tensor_tensor(combine_w[:, :, 1], g_w, e21, ALU.mult))
                dve.wait_ge(sem("place_mm"), at("place_mm", l + 1))
                then(nc.vector.tensor_copy(position, bank[1][:, 0:128].rearrange("p (j n) -> p j n", j=NJ)))
                then(nc.vector.tensor_copy(count, bank[1][:, 128:160]))
                then(nc.vector.tensor_tensor(passes, spread(count, 2, 7), spread(cst("thresholds")[:, 0:7], 1, 32),
                                             ALU.is_gt))
                then(nc.vector.reduce_sum(blocks_e, passes, axis=AX.X))
                then(nc.vector.tensor_tensor_scan(over_upto, cst("ones")[:, 0:32], blocks_e, 0.0, ALU.mult, ALU.add))
                then(nc.vector.tensor_tensor(over_before, over_upto, blocks_e, ALU.subtract))
                then(nc.vector.tensor_tensor(over_cmp, spread(over_upto, 1, OVER), spread(cst("iota_over")[:, 0:OVER], 2, 32),
                                             ALU.is_le))
                then(nc.vector.reduce_sum(over_expert[:, 0:OVER], over_cmp, axis=AX.X))
                then(nc.vector.tensor_scalar(over_expert[:, 0:OVER], over_expert[:, 0:OVER], float(E - 1), None, ALU.min))
                then(nc.vector.tensor_copy(over_ids[:, 0:OVER], over_expert[:, 0:OVER]))
                then(nc.vector.tensor_copy(ints[:, 136:137], over_upto[:, 31:32]))
                for c, hot in enumerate((hot1, hot2)):
                    for q, what in enumerate((position, iota32, spread(over_before, 1, NJ))):
                        then(nc.vector.tensor_tensor(pick_prod, hot, what, ALU.mult))
                        then(nc.vector.reduce_sum(picked[:, q, :, c], pick_prod, axis=AX.X))
                pos, exp, over = (picked[:, q, :, :].rearrange("p j c -> p (j c)") for q in range(3))
                then(nc.vector.tensor_tensor(level8, spread(pos, 2, 7), spread(cst("thresholds")[:, 0:7], 1, 8),
                                             ALU.is_ge))
                then(nc.vector.reduce_sum(level, level8, axis=AX.X))
                then(nc.vector.scalar_tensor_tensor(row_in, level, -float(CAP), pos, ALU.mult, ALU.add))
                then(nc.vector.tensor_scalar(is_over, level, 1.0, None, ALU.min))
                then(nc.vector.tensor_tensor(block_of, over, exp, ALU.subtract))
                then(nc.vector.scalar_tensor_tensor(block_of, level, float(E - 1), block_of, ALU.add, ALU.add))
                then(nc.vector.tensor_tensor(block_of, block_of, is_over, ALU.mult))
                then(nc.vector.tensor_tensor(block_of, block_of, exp, ALU.add))
                then(nc.vector.scalar_tensor_tensor(slot_f, block_of, float(CAP), row_in, ALU.mult, ALU.add))
                if l:
                    dve.wait_ge(sem("combined"), 8)
                then(nc.vector.tensor_copy(ints[:, 0:8], slot_f))
                then(nc.vector.scalar_tensor_tensor(slot_f, row_in, float(E + OVER), block_of, ALU.mult, ALU.add))
                then(nc.vector.tensor_copy(token_i, cst("token_id")))
                nc.vector.tensor_copy(ints[:, 8:16], slot_f).then_inc(sem("entries_ready"), 1)
                for e in range(E):
                    n = E * l + e

                    def x_out(n):
                        dve.wait_ge(sem("gathered_T"), n + 1)
                        nc.vector.tensor_tensor(xgT[:, n % 2, :, :], bank[2 + n % 2][:, :].rearrange("p (k t) -> p k t", k=NK),
                                                spread(v8(f"m_ln{l}"), 2, CAP), ALU.mult).then_inc(sem("xgT_ready"), 1)
                    if e == 0:
                        x_out(n)
                    if e < E - 1:
                        dve.wait_ge(sem("hidden_mm"), n)
                        x_out(n + 1)
                    dve.wait_ge(sem("silu"), n + 1)
                    if n >= 2:
                        dve.wait_ge(sem("gated_T"), n - 1)
                    nc.vector.tensor_tensor(gated[:, n % 2, :], silu_h[:, n % 2, :], bank[4 + n % 2][:, 256:512],
                                            ALU.mult).then_inc(sem("gated_ready"), 1)
                    dve.wait_ge(sem("gated_T"), n + 1)
                    if n >= 2:
                        dve.wait_ge(sem("expert_mm"), n - 1)
                    nc.vector.tensor_copy(hT[:, n % 2, :, :, :], bank[n % 2][:, 0:256].rearrange("p (i q t) -> p i q t", i=2, q=2)
                                          ).then_inc(sem("h_ready"), 1)
                n_over = dve.value_load(over_count, min_val=0, max_val=OVER)
                with dve.If(n_over > 0):
                    dve.wait_ge(sem("y_store0"), 512 * (l + 1))
                    with dve.Fori(0, n_over) as b:
                        dve.wait_ge(sem(f"over_pe{l}"), 4 * b + 1)
                        nc.vector.tensor_tensor(xgT[:, 0, :, :], bank[2][:, :].rearrange("p (k t) -> p k t", k=NK),
                                                spread(v8(f"m_ln{l}"), 2, CAP), ALU.mult).then_inc(sem(f"over_dve{l}"), 1)
                        dve.wait_ge(sem(f"over_act{l}"), b + 1)
                        nc.vector.tensor_tensor(gated[:, 0, :], silu_h[:, 0, :], bank[4][:, 256:512],
                                                ALU.mult).then_inc(sem(f"over_dve{l}"), 1)
                        dve.wait_ge(sem(f"over_pe{l}"), 4 * b + 3)
                        nc.vector.tensor_copy(hT[:, 0, :, :, :], bank[0][:, 0:256].rearrange("p (i q t) -> p i q t", i=2, q=2)
                                              ).then_inc(sem(f"over_dve{l}"), 1)
                        dve.wait_ge(sem(f"over_pe{l}"), 4 * b + 4)
                        nc.vector.tensor_copy(yb[:, 0, :], bank[6][:, :]).then_inc(sem(f"over_dve{l}"), 1)
                        dve.wait_ge(sem(f"over_store{l}"), 32 * b + 32)
                for j in range(NJ):
                    for c in range(2):
                        q = 2 * j + c
                        dve.wait_ge(sem(f"y_got{q % 4}"), 16 * (2 * l + q // 4 + 1))
                        if q:
                            dve.wait_ge(sem("combined"), 8 * l + q)
                        nc.vector.scalar_tensor_tensor(h[:, j, :], y_got[:, q % 4, :], combine_w[:, j, c:c + 1], h[:, j, :],
                                                       ALU.mult, ALU.add).then_inc(sem("combined"), 1)

            dve.wait_ge(sem("h_rwkv"), 8)
            moe_dve(0)
            norm_scale(2, xn_m)
            for k in range(1, NK, 2):
                dve.wait_ge(sem("tr_done"), 16 + k + 1)
                nc.vector.tensor_scalar(xT_kv[:, k, :], bank[k][:, :], v8("kv_ln")[:, k:k + 1], None, ALU.mult)
                nc.vector.tensor_scalar(xT_b[:, k, :], bank[k][:, :], v8("b_ln")[:, k:k + 1], None,
                                        ALU.mult).then_inc(sem("xT_dve"), 1)
            dve.wait_ge(sem("expert_mm"), E)
            nc.vector.memset(rel[32:33, :], NEG).then_inc(sem("rel_mask"), 1)
            dve.wait_ge(sem("tr_done"), 24)
            for u in range(1, 12, 2):
                dve.wait_ge(sem("kv_mm"), at("kv_mm", u + 1))
                b = bank[u % 8]
                if u < 8:
                    kind = u // 2
                    nc.vector.tensor_copy(keys[kind][0:64, 2, :], b[0:64, :])
                    nc.vector.tensor_copy(keys[kind][64:128, 3, :], b[64:128, :]).then_inc(sem("kv_dve"), 1)
                else:
                    nc.vector.tensor_copy(values[:, u - 8, :, :], b[:, :].rearrange("p (b n) -> p b n", b=2)).then_inc(sem("kv_dve"), 1)
            dve.wait_ge(sem("rev_out"), 16)
            for m in range(1, NP, 2):
                dve.wait_ge(sem("q_mm"), at("q_mm", m + 1))
                nc.vector.tensor_scalar(q_T[:, m, :], bank[m][:, :], HD ** -0.5, None, ALU.mult).then_inc(sem("q_dve"), 1)
            dve.wait_ge(sem("cmp_pe_in"), at("cmp_pe_in", 32))
            dve.wait_ge(sem("keys_in"), 128)
            dve.wait_ge(sem("kv_mm"), at("kv_mm", 12))
            for i in range(2):
                for par in range(2):
                    half = slice(64 * par, 64 * par + 64)
                    for g in range(NG):
                        rows = keys[i][half, g, :]
                        src = bass.AP(tensor=rows.tensor, offset=rows.offset + par,
                                      ap=[[*rows.ap[0]], [2, 16], [16, NCMP]])
                        last = nc.vector.tensor_tensor(blocks_in[i][half, :, g, :], src,
                                                       spread(cmp_pe[i][half, :, g], 2, NCMP), ALU.add)
                last.then_inc(sem("blocks_ready"), 1)
            then(nc.vector.tensor_scalar(cmask, bias_c[:, 0, :], 0.1 * NEG, None, ALU.is_gt))
            dve.wait_ge(sem("cmp_out"), at("cmp_out", 2))
            dve.wait_ge(sem("cmp_zero"), 1)
            for a in range(HPG):
                rows = slice(32 * a, 32 * a + NCMP)
                last = nc.vector.tensor_copy(vcmp_diag[rows, :, HD * a:HD * a + HD],
                                             bank[5][rows, 0:256].rearrange("p (g n) -> p g n", g=NG))
            last.then_inc(sem("vcmp_ready"), 1)
            dve.wait_ge(sem("gates_ready"), at("gates_ready", 1))
            for j in range(NJ):
                lo = 24 - 8 * j
                w = cprobs[:, j % 2, :, 0:NCMP]
                dve.wait_ge(sem("cS_mm"), at("cS_mm", j + 1))
                if j >= 2:
                    dve.wait_ge(sem("cT_mm"), at("cT_mm", j - 1))
                for par in range(2):
                    s = bank[2 * (j % 2) + par][:, 0:256].rearrange("p (h k) -> p h k", h=NH // 2)
                    last = nc.vector.tensor_tensor(w[:, par::2, :], s[:, :, 0:NCMP], bias_c[:, par::2, lo:lo + NCMP], ALU.add)
                then(last)
                then(nc.vector.reduce_max(cmax, w, axis=AX.X))
                nc.vector.tensor_tensor(w, w, spread(cmax, 2, NCMP), ALU.subtract).then_inc(sem("cshifted"), 1)
                dve.wait_ge(sem("cexp"), at("cexp", j + 1))
                then(nc.vector.tensor_tensor(w, w, spread(cmask[:, lo:lo + NCMP], 1, NH), ALU.mult))
                then(nc.vector.reduce_sum(csum, w, axis=AX.X))
                then(nc.vector.tensor_scalar(csum, csum, 1e-30, None, ALU.max))
                then(nc.vector.reciprocal(csum, csum))
                then(nc.vector.tensor_tensor(csum, csum, gates[:, j, 0::3], ALU.mult))
                nc.vector.tensor_tensor(w, w, spread(csum, 2, NCMP), ALU.mult).then_inc(sem("cprobs_ready"), 1)
                for g2 in range(2):
                    dve.wait_ge(sem("cO_mm"), at("cO_mm", 2 * j + g2 + 1))
                    nc.vector.tensor_copy(o_rows[:, j, 512 * g2:512 * g2 + 512], bank[7][:, :]).then_inc(sem("cO_ev"), 1)
            dve.wait_ge(sem("cO_ev"), at("cO_ev", 8))
            for tick in range(len(ITEMS) + 3):
                n = tick - 2
                if 0 <= n < len(ITEMS):
                    hh, j = ITEMS[n]
                    dve.wait_ge(sem("probs_mm"), at("probs_mm", n + 1))
                    nc.vector.tensor_copy(probs_T[:, n % 2, 1, 0:P * (j + 1)], bank[5][:, 0:P * (j + 1)]).then_inc(sem("pT_dve"), 1)
                n = tick - 2
                if 0 <= n < len(ITEMS):
                    hh, j = ITEMS[n]
                    then(nc.vector.reciprocal(share[:, n % 3, :], total[:, n % 3, :]))
                    then(nc.vector.tensor_tensor(share[:, n % 3, :], share[:, n % 3, :], gates[:, j, 3 * hh + 1:3 * hh + 3],
                                                 ALU.mult))
                n = tick - 3
                if n >= 0:
                    hh, j = ITEMS[n]
                    o = o_rows[:, j, HD * hh:HD * hh + HD]
                    dve.wait_ge(sem("O_mm"), at("O_mm", n + 1))
                    then(nc.vector.scalar_tensor_tensor(o, bank[6 + n % 2][:, 0:64], share[:, n % 3, 0:1], o, ALU.mult, ALU.add))
                    nc.vector.scalar_tensor_tensor(o, bank[6 + n % 2][:, 64:128], share[:, n % 3, 1:2], o, ALU.mult,
                                                   ALU.add).then_inc(sem("o_added"), 1)
                n = tick
                if n < len(ITEMS):
                    hh, j = ITEMS[n]
                    dve.wait_ge(sem("S_mm"), at("S_mm", n + 1))
                    if j == 0:
                        dve.wait_ge(sem(f"bias_h{hh % 4}"), at(f"bias_h{hh % 4}", 16 * (hh // 4 + 1)))
                    if n >= 3:
                        dve.wait_ge(sem("probs_mm"), at("probs_mm", n - 2))
                    for b in range(2):
                        last = nc.vector.tensor_tensor_reduce(
                            out=probs[:, n % 3, b, 0:P * (j + 1)], in0=bank[2 * (n % 2) + b][:, 0:P * (j + 1)],
                            in1=bias_h[:, hh % 4, 384 - P * j:512], scale=1.0, scalar=3 * NEG, op0=ALU.add, op1=ALU.max,
                            accum_out=top[:, n % 3, b:b + 1])
                    then(last)
                    nc.vector.tensor_scalar(top[:, n % 3, :], top[:, n % 3, :], -1.0, None, ALU.mult).then_inc(sem("biased"), 1)
            for m in range(1, NP, 2):
                dve.wait_ge(sem("oT_mm"), at("oT_mm", m + 1))
                nc.vector.tensor_copy(o_T[:, m, :], bank[m][:, :]).then_inc(sem("oT_dve"), 1)
            for j in range(NJ):
                for q in range(2):
                    dve.wait_ge(sem("b_wo_mm"), at("b_wo_mm", 2 * j + q + 1))
                    nc.vector.tensor_tensor(h[:, j, 512 * q:512 * q + 512], bank[2 * j + q][:, :],
                                            h[:, j, 512 * q:512 * q + 512], ALU.add).then_inc(sem("h_nsa"), 1)
            moe_dve(1)
            dve.wait_ge(sem("norm_sq"), 5)
            nc.vector.tensor_scalar(sumsq, sumsq, 1.0 / D, EPS, ALU.mult, ALU.add).then_inc(sem("norm_var"), 1)
            dve.wait_ge(sem("norm_std"), 5)
            nc.vector.reciprocal(rstd, rstd).then_inc(sem("norm_rstd"), 1)
            dve.wait_ge(sem("norm_rstd"), 5)
            dve.wait_ge(sem("final_in"), 16)
            for j in range(NJ):
                nc.vector.scalar_tensor_tensor(xn_m[:, j, :], h[:, j, :], rstd[:, j:j + 1], final_gain, ALU.mult,
                                               ALU.mult).then_inc(sem("out_ready"), 1)

        @block.tensor
        def _(pe):
            def mm(dst, lhsT, rhs, start=True, stop=True):
                return nc.tensor.matmul(dst, lhsT, rhs, start=start, stop=stop)

            def norm_transpose(i, xn):
                for k in range(NK):
                    for j in range(NJ):
                        if k == 0:
                            pe.wait_ge(sem("xn_ready"), 4 * i + j + 1)
                        last = nc.tensor.transpose(bank[k][:, P * j:P * j + P], xn[:, j, k::NK], ident)
                    last.then_inc(sem("tr_done"), 1)

            pe.wait_ge(sem("const_in"), 16)
            norm_transpose(0, xn)
            pe.wait_ge(sem("lora1_in"), 48)
            pe.wait_ge(sem("xT_act"), 4)
            pe.wait_ge(sem("xT_dve"), 4)
            for i, parts in enumerate((((bank[0], w1l, 0, 64),), ((bank[1], a1l, 0, 64),),
                                       ((bank[2], g1l, 0, 128), (bank[3], g1l, 128, 160)))):
                for k in range(NK):
                    q = 8 * i + k
                    pe.wait_ge(sem("mix_ready"), q + 1)
                    for b, w, lo, hi in parts:
                        last = mm(b[0:hi - lo, :], w[:, k, lo:hi], mix[:, q % 8, :], k == 0, k == NK - 1)
                    last.then_inc(sem("mix_used"), 1)
                pe.wait_ge(sem("mix_used"), 8 * i + 8)
                pe.sem_inc(sem("lora_hid"), 1)
            pe.wait_ge(sem("lora2_in"), 64)
            for m in range(NP):
                cols = slice(P * m, P * m + P)
                for i in range(3):
                    s = 3 * m + i
                    if m == 0:
                        pe.wait_ge(sem("hid_ev"), i + 1)
                    if s >= 4:
                        pe.wait_ge(sem("lora_ev"), s - 3)
                    b = bank[4 + s % 4]
                    if i == 0:
                        last = mm(b[:, :], w2l[0:64, cols], hid_w[0:64, :])
                    elif i == 1:
                        last = mm(b[:, :], a2l[0:64, cols], hid_a[0:64, :])
                    else:
                        mm(b[:, :], g2l[:, cols], hid_g[:, :], True, False)
                        last = mm(b[:, :], g2r[0:32, cols], hid_r[0:32, :], False, True)
                    last.then_inc(sem("lora_mm"), 1)
            pe.wait_ge(sem("lora_ev"), 24)
            for i in range(3):
                for k in range(NK):
                    q = 8 * i + k
                    pe.wait_ge(sem("mix_ready"), 24 + q + 1)
                    pe.wait_ge(sem(f"wring{q % 4}"), 16 * (q // 4 + 1))
                    for m in range(NP):
                        if k == 0 and i == 1:
                            pe.wait_ge(sem("proj_ev"), m + 1)
                        if k == 0 and i == 2:
                            pe.wait_ge(sem("k_norm2"), m + 1)
                        last = mm(bank[m][:, :], wring[:, q % 4, P * m:P * m + P], mix[:, q % 8, :], k == 0, k == NK - 1)
                        if k == NK - 1 and m < NP - 1:
                            last.then_inc(sem("proj_mm"), 1)
                    last.then_inc(sem("mix_used"), 1)
                pe.wait_ge(sem("mix_used"), 24 + 8 * i + 8)
                pe.sem_inc(sem("proj_mm"), 1)
                if i == 1:
                    for m in range(NP):
                        pe.wait_ge(sem("proj_ev"), 8 + m + 1)
                        pe.wait_ge(sem("k_sq"), m + 1)
                        mm(bank[m][:, :], head_ones, a_T[:, m, :]).then_inc(sem("k_ssq"), 1)
            for m in range(NP):
                pe.wait_ge(sem("proj_ev"), 16 + m + 1)
                pe.wait_ge(sem("rk_ready"), m + 1)
                mm(bank[m][:, :], head_ones, tmp[:, 3, m % 2, :]).then_inc(sem("bonus_mm"), 1)

            pe.wait_ge(sem("bonus_ev"), NP)
            for tick in range(PACKS + 11):
                def pack(off):
                    n = tick - off
                    return n if 0 <= n < PACKS else None

                if (n := pack(0)) is not None:
                    m, c = n % NP, n // NP
                    pe.wait_ge(sem("ex_ab"), n + 1)
                    if n - 1 >= 0:
                        pe.wait_ge(sem("ev_g"), upto(n - 1))
                    if tick - 9 >= 0:
                        pe.wait_ge(sem("ev_rh"), upto(tick - 9))
                    e = ab_e[:, n % 2, :]
                    mm(p_g, e[:, 128:256], a_T[:, m, c * C:c * C + C])
                    mm(p_a, e[:, 0:128], e[:, 128:256]).then_inc(sem("pe_g"), 1)
                if (n := pack(1)) is not None:
                    pe.wait_ge(sem("ev_g"), n + 1)
                    if n - 1 >= 0:
                        pe.wait_ge(sem("ev_sq"), upto(n - 1))
                    if tick - 10 >= 0:
                        pe.wait_ge(sem("ev_u"), upto(tick - 10))
                    mm(p_sq[:, 0:128], a32[:, n % 2, :], at32[:, n % 2, :])
                    mm(p_sq[:, 128:256], at32[:, n % 2, :], a32[:, n % 2, :]).then_inc(sem("pe_sq"), 1)
                for lvl, off, ps in ((1, 2, p_l1), (2, 3, p_l2)):
                    if (n := pack(off)) is not None:
                        pe.wait_ge(sem("ev_sq" if lvl == 1 else "ev_l1"), n + 1)
                        pe.wait_ge(sem("ev_x" + str(lvl - 1)), n + 1)
                        if n - 1 >= 0:
                            pe.wait_ge(sem(f"ev_l{lvl}"), upto(n - 1))
                        x = lv[lvl][:, n % 2, :]
                        mm(ps[:, 0:256], x[:, 256:384], x[:, 0:256])
                        mm(ps[:, 256:384], x[:, 128:256], x[:, 256:384]).then_inc(sem(f"pe_l{lvl}"), 1)
                if (n := pack(4)) is not None:
                    pe.wait_ge(sem("ev_l2"), n + 1)
                    pe.wait_ge(sem("ev_x2"), n + 1)
                    if n - 1 >= 0:
                        pe.wait_ge(sem("ev_l3"), upto(n - 1))
                    if tick - 11 >= 0:
                        pe.wait_ge(sem("ev_y"), upto(tick - 11))
                    x = lv[3][:, n % 2, :]
                    mm(p_l3[:, 0:128], x[:, 256:384], x[:, 0:128])
                    mm(p_l3[:, 128:256], x[:, 128:256], x[:, 256:384]).then_inc(sem("pe_l3"), 1)
                if (n := pack(5)) is not None:
                    pe.wait_ge(sem("ev_l3"), n + 1)
                    pe.wait_ge(sem("ev_x3"), n + 1)
                    if n - 1 >= 0:
                        pe.wait_ge(sem("ev_x4"), upto(n - 1))
                    if tick - 8 >= 0:
                        pe.wait_ge(sem("ev_tr"), upto(tick - 8))
                    x = lv[4][:, n % 2, :]
                    mm(p_l4, x[:, 128:256], x[:, 0:128]).then_inc(sem("pe_l4"), 1)
                if (n := pack(6)) is not None:
                    pe.wait_ge(sem("ev_x4"), n + 1)
                    if n - 1 >= 0:
                        pe.wait_ge(sem("ev_mz"), upto(n - 1))
                    if tick - 8 >= 0:
                        pe.wait_ge(sem("ev_late"), upto(tick - 8))
                    nc.tensor.transpose(p_mz[:, 0:128], x4[:, n % 4, :], ident)
                    mm(p_mz[:, 128:256], a_off[:, n % 8, :], x4[:, n % 4, :]).then_inc(sem("pe_mz"), 1)
                if (n := pack(7)) is not None:
                    m, c = n % NP, n // NP
                    pe.wait_ge(sem("ev_mz"), n + 1)
                    if n - 1 >= 0:
                        pe.wait_ge(sem("ev_mx"), upto(n - 1))
                    if tick - 11 >= 0:
                        pe.wait_ge(sem("ev_s"), upto(tick - 11))
                    mm(p_mx, tz[:, n % 2, 0:128], tz[:, n % 2, 128:256]).then_inc(sem("pe_mx"), 1)
                if (n := pack(8)) is not None:
                    m, c = n % NP, n // NP
                    pe.wait_ge(sem("ev_tr"), n + 1)
                    pe.wait_ge(sem("ev_late"), n + 1)
                    if c:
                        pe.wait_ge(sem("ev_s"), n - NP + 1)
                    else:
                        pe.wait_ge(sem("state_zero"), 1)
                    if n - 1 >= 0:
                        pe.wait_ge(sem("ev_rh"), upto(n - 1))
                    if tick >= 0:
                        pe.wait_ge(sem("ev_g"), upto(tick))
                    mm(p_rh, a_e[:, n % 4, :], state[:, m, :], True, False)
                    mm(p_rh, ak_t[:, n % 4, :], bkv_s[:, n % 4, 256:384], False, True).then_inc(sem("pe_rh"), 1)
                if (n := pack(9)) is not None:
                    pe.wait_ge(sem("ev_rh"), n + 1)
                    pe.wait_ge(sem("ev_mx"), n + 1)
                    if n - 1 >= 0:
                        pe.wait_ge(sem("ev_u"), upto(n - 1))
                    if tick - 1 >= 0:
                        pe.wait_ge(sem("ev_sq"), upto(tick - 1))
                    mm(p_u, x_all[:, n % 4, :], rhs_s[:, n % 2, :]).then_inc(sem("pe_u"), 1)
                if (n := pack(10)) is not None:
                    m, c = n % NP, n // NP
                    pe.wait_ge(sem("ev_u"), n + 1)
                    if n - 1 >= 0:
                        pe.wait_ge(sem("ev_y"), upto(n - 1))
                    if tick - 4 >= 0:
                        pe.wait_ge(sem("ev_l3"), upto(tick - 4))
                    s4 = bkv_s[:, n % 4, :]
                    mm(p_y, state[:, m, :], r_T[:, m, c * C:c * C + C], True, False)
                    mm(p_y, u_s[:, n % 4, :], rbk[:, n % 4, 0:64], False, False)
                    mm(p_y, s4[:, 256:384], rbk[:, n % 4, 64:128], False, True).then_inc(sem("pe_y"), 1)
                if (n := pack(7)) is not None:
                    m, c = n % NP, n // NP
                    pe.wait_ge(sem("ex_late"), n + 1)
                    if n - 1 >= 0:
                        pe.wait_ge(sem("ev_tr"), upto(n - 1))
                    if tick - 5 >= 0:
                        pe.wait_ge(sem("ev_x4"), upto(tick - 5))
                    if n - 1 >= 0:
                        pe.wait_ge(sem("ev_late"), upto(n - 1))
                    if tick - 6 >= 0:
                        pe.wait_ge(sem("ev_mz"), upto(tick - 6))
                    e = bkv_e[:, n % 2, :]
                    cs = slice(c * C, c * C + C)
                    for i in range(3):
                        nc.tensor.transpose(p_tr[:, P * i:P * i + P], e[:, P * i:P * i + P], ident)
                    mm(p_late[:, 0:64], e[:, 0:128], r_T[:, m, cs])
                    mm(p_late[:, 64:192].rearrange("p (w t) -> p w t", w=2), e[:, 128:256],
                       ra_T[:, :, m, cs]).then_inc(sem("pe_tr"), 1)
                if (n := pack(10)) is not None:
                    s4 = bkv_s[:, n % 4, :]
                    if n - 1 >= 0:
                        pe.wait_ge(sem("ev_s"), upto(n - 1))
                    if tick - 7 >= 0:
                        pe.wait_ge(sem("ev_mx"), upto(tick - 7))
                    mm(p_s, s4[:, 0:128], u_s[:, n % 4, :], True, False)
                    mm(p_s, s4[:, 128:256], s4[:, 256:384], False, True).then_inc(sem("pe_s"), 1)

            pe.wait_ge(sem("ev_y"), PACKS)
            pe.wait_ge(sem("ev_s"), PACKS)
            for m in range(NP):
                if m >= 4:
                    pe.wait_ge(sem("y_centered"), m - 3)
                mm(bank[m % 4][:, :], head_ones, y_T[:, m, :]).then_inc(sem("y_mean"), 1)
            for m in range(NP):
                pe.wait_ge(sem("y_sq"), m + 1)
                if m >= 4:
                    pe.wait_ge(sem("y_var"), m - 3)
                mm(bank[4 + m % 4][:, :], head_ones, r_T[:, m, :]).then_inc(sem("y_ssq"), 1)
            pe.wait_ge(sem("y_var"), NP)
            for m in range(NP):
                q = 24 + m
                pe.wait_ge(sem("y_ready"), m + 1)
                pe.wait_ge(sem(f"wring{q % 4}"), 16 * (q // 4 + 1))
                for b in range(8):
                    last = mm(bank[b][:, :], y_T[:, m, P * (b // 2):P * (b // 2) + P],
                              wring[:, q % 4, 512 * (b % 2):512 * (b % 2) + 512], m == 0, m == NP - 1)
                    if m == NP - 1:
                        last.then_inc(sem("wo_mm"), 1)
                if m < NP - 1:
                    last.then_inc(sem("wo_used"), 1)
            def moe_pe(l):
                i = 1 + 2 * l
                norm_transpose(i, xn_m)
                pe.wait_ge(sem("router_in"), 32)
                pe.wait_ge(sem("xT_act"), 4 * (i + 1))
                pe.wait_ge(sem("xT_dve"), 4 * (i + 1))
                for j in range(NJ):
                    for k in range(NK):
                        last = mm(bank[0][:, 64 * j:64 * j + 36], xT_m[:, k, P * j:P * j + P], router_w[:, l, k, :],
                                  k == 0, k == NK - 1)
                last.then_inc(sem("router_mm"), 1)
                pe.wait_ge(sem("two_hot"), l + 1)
                for j in range(NJ + 1):
                    for q in range(min(j + 1, NJ)):
                        last = mm(bank[1][:, 32 * j:32 * j + 32], cst("before") if q == j else cst("ones"),
                                  two_hot[:, q, :], q == 0, q == min(j, NJ - 1))
                last.then_inc(sem("place_mm"), 1)

                def transpose_rows(n):
                    pe.wait_ge(sem(f"gather{n % 2}"), 16 * (n // 2 + 1))
                    if n >= 2:
                        pe.wait_ge(sem("xgT_ready"), n - 1)
                    for k in range(NK):
                        last = nc.tensor.transpose(bank[2 + n % 2][:, CAP * k:CAP * k + CAP], xg[:, n % 2, k::NK],
                                                   ident[0:CAP, 0:CAP])
                    last.then_inc(sem("gathered_T"), 1)

                def hidden(slot, w13, done):
                    for k in range(NK):
                        for q in range(2):
                            last = mm(bank[4 + slot][CAP * q:CAP * q + CAP, :].rearrange("p (w n) -> p w n", w=2),
                                      xgT[:, slot, k, :], w13[:, :, k, 256 * q:256 * q + 256], k == 0, k == NK - 1)
                    last.then_inc(sem(done), 1)

                def transpose_gated(slot, done):
                    for i in range(2):
                        last = nc.tensor.transpose(bank[slot][:, P * i:P * i + P], gated[:, slot, P * i:P * i + P], ident)
                    last.then_inc(sem(done), 1)

                def result(slot, w2, done):
                    for c in range(4):
                        for q in range(2):
                            last = mm(bank[6 + slot][CAP * q:CAP * q + CAP, :], hT[:, slot, c % 2, c // 2, :],
                                      w2[:, c, 512 * q:512 * q + 512], c == 0, c == 3)
                    last.then_inc(sem(done), 1)

                transpose_rows(E * l)
                for e in range(E):
                    n = E * l + e
                    pe.wait_ge(sem("xgT_ready"), n + 1)
                    if n >= 2:
                        pe.wait_ge(sem("gated_ready"), n - 1)
                    pe.wait_ge(sem(f"w0_in{n % 3}"), 16 * (n // 3 + 1))
                    pe.wait_ge(sem(f"w1_in{n % 3}"), 16 * (n // 3 + 1))
                    hidden(n % 2, w13_slot[n % 3], "hidden_mm")
                    if e < E - 1:
                        transpose_rows(n + 1)
                    pe.wait_ge(sem("gated_ready"), n + 1)
                    if n >= 2:
                        pe.wait_ge(sem("h_ready"), n - 1)
                    transpose_gated(n % 2, "gated_T")
                    pe.wait_ge(sem("h_ready"), n + 1)
                    pe.wait_ge(sem(f"w2_in{n % 3}"), 16 * (n // 3 + 1))
                    if n >= 2:
                        pe.wait_ge(sem("yb_ready"), n - 1)
                    result(n % 2, w_slot[n % 3][2].rearrange("p (k n) -> p k n", k=4), "expert_mm")
                n_over = pe.value_load(over_count, min_val=0, max_val=OVER)
                with pe.If(n_over > 0):
                    pe.wait_ge(sem("yb_ready"), E * (l + 1))
                    with pe.Fori(0, n_over) as b:
                        pe.wait_ge(sem(f"over_x{l}"), 16 * b + 16)
                        pe.sem_inc(sem("over_turn_pe"), 1)
                        for k in range(NK):
                            last = nc.tensor.transpose(bank[2][:, CAP * k:CAP * k + CAP], xg[:, 0, k::NK],
                                                       ident[0:CAP, 0:CAP])
                        last.then_inc(sem(f"over_pe{l}"), 1)
                        pe.wait_ge(sem(f"over_w{l}"), 48 * b + 48)
                        pe.wait_ge(sem(f"over_dve{l}"), 4 * b + 1)
                        hidden(0, w13_slot[1], f"over_pe{l}")
                        pe.wait_ge(sem(f"over_dve{l}"), 4 * b + 2)
                        transpose_gated(0, f"over_pe{l}")
                        pe.wait_ge(sem(f"over_dve{l}"), 4 * b + 3)
                        result(0, w_slot[1][2].rearrange("p (k n) -> p k n", k=4), f"over_pe{l}")
                        pe.wait_ge(sem(f"over_dve{l}"), 4 * b + 4)

            moe_pe(0)
            norm_transpose(2, xn_m)
            pe.wait_ge(sem("kv_w_in"), at("kv_w_in", 16))
            pe.wait_ge(sem("xT_act"), 12)
            pe.wait_ge(sem("xT_dve"), 12)
            for u in range(12):
                if u >= 8:
                    evacuated = "kv_dve" if u % 2 else "kv_act"
                    pe.wait_ge(sem(evacuated), at(evacuated, (u - 8) // 2 + 1))
                if u < 8:
                    col = 256 * (0, 1, 2, 4)[u // 2] + P * (u % 2)
                    for k in range(NK):
                        last = mm(bank[u % 8][:, :], w_kv[:, k, col:col + P], xT_kv[:, k, :], k == 0, k == NK - 1)
                else:
                    j = u - 8
                    for b, col in enumerate((768, 1280)):
                        for k in range(NK):
                            last = mm(bank[u % 8][:, 256 * b:256 * b + 256], xT_kv[:, k, P * j:P * j + P],
                                      w_kv[:, k, col:col + 256], k == 0, k == NK - 1)
                last.then_inc(sem("kv_mm"), 1)
            pe.wait_ge(sem("bias_in"), at("bias_in", 48))
            pe.wait_ge(sem("rel_mask"), at("rel_mask", 1))
            pe.wait_ge(sem("kv_act"), at("kv_act", 4))
            pe.wait_ge(sem("kv_dve"), at("kv_dve", 4))
            for m in range(NOFF):
                mm(bank[4 + m // 32][:, 16 * (m % 32):16 * (m % 32) + 16], fwd[:, 864 - 16 * m:992 - 16 * m], rel)
            mm(bank[6][0:NH, :], rel, rev[:, 0:512])
            mm(bank[7][0:NH, 0:128], rel, rev[:, 512:640]).then_inc(sem("bias_mm"), 1)
            pe.wait_ge(sem("q_w_in"), at("q_w_in", 16))
            for m in range(NP):
                if m == 0:
                    pe.wait_ge(sem("kv_act"), at("kv_act", 6))
                    pe.wait_ge(sem("kv_dve"), at("kv_dve", 6))
                if m == 4:
                    pe.wait_ge(sem("rev_ev"), at("rev_ev", 1))
                for k in range(NK):
                    last = mm(bank[m][:, :], w_q[:, k, P * m:P * m + P], xT_b[:, k, :], k == 0, k == NK - 1)
                last.then_inc(sem("q_mm"), 1)
            pe.wait_ge(sem("gate_w_in"), at("gate_w_in", 16))
            pe.wait_ge(sem("q_act"), at("q_act", 1))
            for j in range(NJ):
                for k in range(NK):
                    last = mm(bank[0][:, 64 * j:64 * j + 48], xT_b[:, k, P * j:P * j + P], w_gate[:, k, :],
                              k == 0, k == NK - 1)
            last.then_inc(sem("gate_mm"), 1)
            pe.wait_ge(sem("cmp_w1_in"), at("cmp_w1_in", 32))
            pe.wait_ge(sem("q_act"), at("q_act", 4))
            pe.wait_ge(sem("q_dve"), at("q_dve", 4))
            for i in range(2):
                pe.wait_ge(sem("blocks_ready"), at("blocks_ready", i + 1))
                for s in range(2):
                    for m in range(16):
                        last = mm(bank[2 + i][:, P * s:P * s + 124], cmp_w1[i][:, m, P * s:P * s + P],
                                  blocks_in[i][:, m, :, :], m == 0, m == 15)
                last.then_inc(sem("cmp_hidden"), 1)
            pe.wait_ge(sem("cmp_w2_in"), at("cmp_w2_in", 32))
            pe.wait_ge(sem("cmp_act"), at("cmp_act", 1))
            for s in range(2):
                last = mm(bank[4][:, 0:124], cmp_w2[0][:, s, :], cmp_h[0][:, s, 0:124], s == 0, s == 1)
            last.then_inc(sem("cmp_out"), 1)
            pe.wait_ge(sem("cmp_act"), at("cmp_act", 2))
            for a in range(HPG):
                for g in range(NG):
                    for s in range(2):
                        last = mm(bank[5][32 * a:32 * a + NCMP, HD * g:HD * g + HD],
                                  cmp_h[1][:, s, NCMP * g:NCMP * g + NCMP], cmp_w2[1][:, s, :], s == 0, s == 1)
            last.then_inc(sem("cmp_out"), 1)
            pe.wait_ge(sem("kcmp_ready"), at("kcmp_ready", 1))
            pe.wait_ge(sem("gates_ready"), at("gates_ready", 1))
            for j in range(NJ + 1):
                if j < NJ:
                    if j >= 2:
                        pe.wait_ge(sem("cshifted"), at("cshifted", j - 1))
                    for hh in range(NH):
                        half = slice(64 * (hh % 2), 64 * (hh % 2) + 64)
                        last = mm(bank[2 * (j % 2) + hh % 2][:, 32 * (hh // 2):32 * (hh // 2) + NCMP], q_T[half, hh // 2, P * j:P * j + P],
                                  kcmp_T[half, hh // HPG, :])
                    last.then_inc(sem("cS_mm"), 1)
                if j:
                    j = j - 1
                    pe.wait_ge(sem("cprobs_ready"), at("cprobs_ready", j + 1))
                    if j:
                        pe.wait_ge(sem("cT_ready"), at("cT_ready", j))
                    for g in range(NG):
                        last = nc.tensor.transpose(bank[6][:, P * g:P * g + P],
                                                   cprobs[:, j % 2, 4 * g:4 * g + 4, :].rearrange("p h k -> p (h k)"), ident)
                    last.then_inc(sem("cT_mm"), 1)
                    pe.wait_ge(sem("cT_ready"), at("cT_ready", j + 1))
                    pe.wait_ge(sem("vcmp_ready"), at("vcmp_ready", 1))
                    for g2 in range(2):
                        if j or g2:
                            pe.wait_ge(sem("cO_ev"), at("cO_ev", 2 * j + g2))
                        for g in range(2):
                            last = mm(bank[7][:, 256 * g:256 * g + 256], cprobs_T[:, 4 * j + 2 * g2 + g, :],
                                      vcmp_diag[:, 2 * g2 + g, :])
                        last.then_inc(sem("cO_mm"), 1)
            pe.wait_ge(sem("keys_in"), 128)
            pe.wait_ge(sem("cO_ev"), at("cO_ev", 8))
            for tick in range(len(ITEMS) + 2):
                n = tick - 2
                if n >= 0:
                    hh, j = ITEMS[n]
                    pe.wait_ge(sem("probs_ready"), at("probs_ready", n + 1))
                    if n:
                        pe.wait_ge(sem("pT_act"), at("pT_act", n))
                        pe.wait_ge(sem("pT_dve"), at("pT_dve", n))
                    for b in range(2):
                        for s in range(j + 1):
                            last = nc.tensor.transpose(bank[4 + b][:, P * s:P * s + P], probs[:, n % 3, b, P * s:P * s + P],
                                                       ident)
                    last.then_inc(sem("probs_mm"), 1)
                n = tick
                if n < len(ITEMS):
                    hh, j = ITEMS[n]
                    half = slice(64 * (hh % 2), 64 * (hh % 2) + 64)
                    if n >= 2:
                        pe.wait_ge(sem("biased"), at("biased", n - 1))
                    for b in range(2):
                        last = mm(bank[2 * (n % 2) + b][:, 0:P * (j + 1)], q_T[half, hh // 2, P * j:P * j + P],
                                  keys[2 + b][half, hh // HPG, 0:P * (j + 1)])
                    last.then_inc(sem("S_mm"), 1)
                n = tick - 2
                if n >= 0:
                    hh, j = ITEMS[n]
                    pe.wait_ge(sem("pT_act"), at("pT_act", n + 1))
                    pe.wait_ge(sem("pT_dve"), at("pT_dve", n + 1))
                    if n >= 2:
                        pe.wait_ge(sem("o_added"), at("o_added", n - 1))
                    for b in range(2):
                        for s in range(j + 1):
                            last = mm(bank[6 + n % 2][:, 64 * b:64 * b + 64], probs_T[:, n % 2, b, P * s:P * s + P],
                                      values[:, s, b, HD * (hh // HPG):HD * (hh // HPG) + HD], s == 0, s == j)
                    last.then_inc(sem("O_mm"), 1)
            pe.wait_ge(sem("o_added"), at("o_added", len(ITEMS)))
            for m in range(NP):
                for j in range(NJ):
                    last = nc.tensor.transpose(bank[m][:, P * j:P * j + P], o_rows[:, j, P * m:P * m + P], ident)
                last.then_inc(sem("oT_mm"), 1)
            pe.wait_ge(sem("b_wo_in"), at("b_wo_in", 16))
            pe.wait_ge(sem("oT_act"), at("oT_act", 4))
            pe.wait_ge(sem("oT_dve"), at("oT_dve", 4))
            for b in range(8):
                for m in range(NP):
                    last = mm(bank[b][:, :], o_T[:, m, P * (b // 2):P * (b // 2) + P],
                              w_o[:, m, 512 * (b % 2):512 * (b % 2) + 512], m == 0, m == NP - 1)
                last.then_inc(sem("b_wo_mm"), 1)
            moe_pe(1)


def shape_constants():
    import math
    import numpy as np
    i = np.arange(P)
    row, col = i[:, None], i[None, :]
    same = row // HD == col // HD
    half = row // 32 == col // 32
    step, at = row % C, col % C
    parts = {
        "ident": row == col,
        "head_ones": same,
        "upper32": same & half & (step < at),
        "upper64": same & (step < at),
        "upper_incl": step <= at,
        "lower32": same & half & (step > at),
        "lower_off": same & ~half & (step > at),
        "scan_keep": np.broadcast_to(np.arange(T) % C != 0, (P, T)),
        "before": row < col,
        "ones": np.ones((P, P)),
        "head_mask": same,
        "iota": np.broadcast_to(np.arange(32), (P, 32)),
        "iota_over": np.broadcast_to(np.arange(16), (P, 16)),
        "thresholds": np.broadcast_to(CAP * (1 + np.arange(8)), (P, 8)),
        "slot0": np.broadcast_to(CAP * np.arange(32), (P, 32)),
        "token_id": row + P * np.arange(4)[None, :],
    }
    consts = np.concatenate([np.asarray(parts[name], np.float32).reshape(P, n) for name, n in CONST], 1)

    def bucket(dist):
        n = np.maximum(dist, 0)
        big = 16 + (np.log(np.maximum(n, 1).astype(np.float32) / np.float32(16)) / np.float32(math.log(8.0))
                    * np.float32(16)).astype(np.int32)
        return np.where(n < 16, n, np.minimum(big, 31))

    def one_hot(dist):
        rows = (bucket(dist)[None, :] == np.arange(32)[:, None]) & (dist >= 0)[None, :]
        return np.concatenate([rows, (dist < 0)[None, :]]).astype(np.float32)

    return consts, one_hot(511 - np.arange(640)), one_hot(np.arange(1024) - 511)


def kernel(**inputs):
    import numpy as np
    import concourse.bacc as bacc
    from concourse.bass_utils import run_bass_kernel_spmd

    a = {k: np.asarray(v) for k, v in inputs.items()}
    x = {k: a[k][0] for k in ("x", "a_wr", "a_wk", "a_wv", "a_wo", "a_w1", "a_w2", "a_a1", "a_a2", "a_g1", "a_g2",
                              "b_wqg", "b_wo")}
    x["cmp_k_w2x2"] = np.concatenate([a["cmp_k_w2"]] * 2, 1)
    x |= {k: a[k] for k in ("kv_w", "cmp_k_w1", "cmp_v_w1", "cmp_v_w2", "rel_bias", "m_w1", "m_w3",
                            "m_w2", "final_ln")}
    vectors = {"a_ln": a["a_ln"][0], "kv_ln": a["kv_ln"], "b_ln": a["b_ln"][0], "m_ln0": a["m_ln"][0],
               "m_ln1": a["m_ln"][1]} | {f"mu{i}": a["a_mu"][0, i] for i in range(6)}
    by_tile = {"w0": a["a_w0"], "a0": a["a_a0"], "kk": a["a_kk"], "ka": a["a_ka"], "rk": a["a_rk"],
               "lnx_w": a["a_lnx_w"], "lnx_b": a["a_lnx_b"]}
    x["vecs"] = np.concatenate([vectors[n].reshape(P, 8) for n in VEC_P]
                               + [by_tile[n].reshape(8, P).T for n in VEC_M], 1)
    for n in "kv":
        x[f"pe_{n}"] = a[f"cmp_pe_{n}"].reshape(NG, 16, P).transpose(2, 1, 0)
    x["router_w"] = np.concatenate([a["m_wg"], a["m_we"]], 2)
    x["router_b"] = np.broadcast_to(np.concatenate([a["m_bg"], a["m_be"]], 1)[:, None, :], (2, P, 36))
    x["consts"], x["bucket_rev"], x["bucket_fwd"] = shape_constants()

    nc = bacc.Bacc("TRN2", target_bir_lowering=False, num_devices=1)
    arrays, args = {}, {}
    for name, v in x.items():
        arrays[name] = np.ascontiguousarray(v)
        args[name] = nc.dram_tensor(name, v.shape, FP32, kind="ExternalInput").ap()
    out = nc.dram_tensor("out", (T, D), FP32, kind="ExternalOutput").ap()
    decoder_program(nc, args, out)
    r = run_bass_kernel_spmd(nc, [arrays], core_ids=[0])
    return r.results[0]["out"].reshape(1, T, D)
```
